# Optimizing a Trainium2 kernel written in Bass

```python
import jax, jax.numpy as jnp
from jax import lax
import numpy as np

D_MODEL = 1024
BATCH = 1
SEQ = 512
DEPTH = 1

PLE_DIM = 256
ROPE_THETA = 10000.0
EPS = 1e-6
NEG_INF = -1e30

MLA_HEADS = 8
MLA_Q_RANK = 384
MLA_KV_RANK = 256
MLA_NOPE = 64
MLA_ROPE = 32
MLA_QK = MLA_NOPE + MLA_ROPE
MLA_V = 64
Q_BLOCK = 128

SWA_HEADS = 8
SWA_KV_HEADS = 2
SWA_GROUP = SWA_HEADS // SWA_KV_HEADS
SWA_HD = 64
WINDOW = 128
BAND_BLOCK = 128

OFF_CQ = MLA_Q_RANK
OFF_CKV = OFF_CQ + MLA_KV_RANK
OFF_KR = OFF_CKV + MLA_ROPE
OFF_QS = OFF_KR + SWA_HEADS * SWA_HD
OFF_KS = OFF_QS + SWA_KV_HEADS * SWA_HD
OFF_VS = OFF_KS + SWA_KV_HEADS * SWA_HD
OFF_GA = OFF_VS + D_MODEL
IN_WIDTH = OFF_GA + D_MODEL

N_EXPERTS = 64
TOP_K = 8
N_GROUPS = 8
TOPK_GROUPS = 4
EXPERTS_PER_GROUP = N_EXPERTS // N_GROUPS
EXPERT_FF = 256
SHARED_FF = 256
ROUTED_SCALE = 2.5
MOE_CHUNK = 128

kernel_name = "hybrid_mla_swa_moe_ple_block"

def rmsnorm(x, g):
    xf = x.astype(jnp.float32)
    y = xf * lax.rsqrt(jnp.mean(xf * xf, axis=-1, keepdims=True) + EPS)
    return (y * g.astype(jnp.float32)).astype(x.dtype)

def rope_cos_sin(positions, dim):
    inv = 1.0 / (ROPE_THETA ** (jnp.arange(0, dim, 2, dtype=jnp.float32) / dim))
    ang = positions.astype(jnp.float32)[..., None] * inv
    return jnp.cos(ang), jnp.sin(ang)

def apply_rope(x, cos, sin):
    x1, x2 = jnp.split(x, 2, axis=-1)
    c = cos[:, :, None, :].astype(x.dtype)
    s = sin[:, :, None, :].astype(x.dtype)
    return jnp.concatenate([x1 * c - x2 * s, x2 * c + x1 * s], axis=-1)

def dense_attention(q, k, v, scale):
    B, S, H, dk = q.shape
    nb = S // Q_BLOCK
    qb = q.reshape(B, nb, Q_BLOCK, H, dk).transpose(1, 0, 2, 3, 4)

    def one_block(qblk):
        s = jnp.einsum('bqhd,bkhd->bhqk', qblk, k).astype(jnp.float32) * scale
        pr = jax.nn.softmax(s, axis=-1).astype(v.dtype)
        return jnp.einsum('bhqk,bkhd->bqhd', pr, v)

    o = lax.map(one_block, qb)
    return o.transpose(1, 0, 2, 3, 4).reshape(B, S, H, v.shape[-1])

def banded_gqa_attention(q, k, v, sink, scale):
    B, S, Hq, d = q.shape
    nb = S // BAND_BLOCK
    pad = ((0, 0), (BAND_BLOCK, BAND_BLOCK), (0, 0), (0, 0))
    kp = jnp.pad(k, pad).reshape(B, nb + 2, BAND_BLOCK, SWA_KV_HEADS, d)
    vp = jnp.pad(v, pad).reshape(B, nb + 2, BAND_BLOCK, SWA_KV_HEADS, d)
    kband = jnp.concatenate([kp[:, :-2], kp[:, 1:-1], kp[:, 2:]], axis=2)
    vband = jnp.concatenate([vp[:, :-2], vp[:, 1:-1], vp[:, 2:]], axis=2)
    qb = q.reshape(B, nb, BAND_BLOCK, SWA_KV_HEADS, SWA_GROUP, d)
    s = jnp.einsum('bnqhgd,bnkhd->bnhgqk', qb, kband).astype(jnp.float32) * scale
    qi = jnp.arange(BAND_BLOCK)[:, None]
    kj = jnp.arange(3 * BAND_BLOCK)[None, :]
    rel = kj - BAND_BLOCK - qi
    kpos = jnp.arange(nb)[:, None, None] * BAND_BLOCK - BAND_BLOCK + kj[None]
    valid = (jnp.abs(rel)[None] <= WINDOW) & (kpos >= 0) & (kpos < S)
    s = jnp.where(valid[None, :, None, None], s, NEG_INF)
    sk = sink.astype(jnp.float32).reshape(SWA_KV_HEADS, SWA_GROUP)[None, None, :, :, None, None]
    m = jnp.maximum(jnp.max(s, axis=-1, keepdims=True), sk)
    e = jnp.exp(s - m)
    denom = jnp.sum(e, axis=-1, keepdims=True) + jnp.exp(sk - m)
    pr = (e / denom).astype(v.dtype)
    o = jnp.einsum('bnhgqk,bnkhd->bnqhgd', pr, vband)
    return o.reshape(B, S, Hq * d)

def token_mixers(x, cos_s, sin_s, cos_m, sin_m, g_mix, w_in, b_gate, g_cq, w_uq, g_ckv, w_ukv,
                 g_qn_mla, g_kn_mla, g_qn_swa, g_kn_swa, sink, w_br_mla, w_br_swa, w_out):
    B, S, _ = x.shape
    h = rmsnorm(x, g_mix)
    z = h @ w_in
    c_q, c_kv, k_r, q_s, k_s, v_s, a_mla, a_swa = jnp.split(
        z, [OFF_CQ, OFF_CKV, OFF_KR, OFF_QS, OFF_KS, OFF_VS, OFF_GA], axis=-1)

    q_m = (rmsnorm(c_q, g_cq) @ w_uq).reshape(B, S, MLA_HEADS, MLA_QK)
    kv_m = (rmsnorm(c_kv, g_ckv) @ w_ukv).reshape(B, S, MLA_HEADS, MLA_NOPE + MLA_V)
    k_nope, v_m = jnp.split(kv_m, [MLA_NOPE], axis=-1)
    k_rope = jnp.broadcast_to(k_r[:, :, None, :], (B, S, MLA_HEADS, MLA_ROPE))
    q_m = rmsnorm(q_m, g_qn_mla)
    k_m = rmsnorm(jnp.concatenate([k_nope, k_rope], axis=-1), g_kn_mla)
    q_m = jnp.concatenate([q_m[..., :MLA_NOPE], apply_rope(q_m[..., MLA_NOPE:], cos_m, sin_m)], axis=-1)
    k_m = jnp.concatenate([k_m[..., :MLA_NOPE], apply_rope(k_m[..., MLA_NOPE:], cos_m, sin_m)], axis=-1)
    o_m = dense_attention(q_m, k_m, v_m, MLA_QK ** -0.5).reshape(B, S, MLA_HEADS * MLA_V)

    q_w = apply_rope(rmsnorm(q_s.reshape(B, S, SWA_HEADS, SWA_HD), g_qn_swa), cos_s, sin_s)
    k_w = apply_rope(rmsnorm(k_s.reshape(B, S, SWA_KV_HEADS, SWA_HD), g_kn_swa), cos_s, sin_s)
    v_w = v_s.reshape(B, S, SWA_KV_HEADS, SWA_HD)
    o_w = banded_gqa_attention(q_w, k_w, v_w, sink, SWA_HD ** -0.5)

    gate_m = jax.nn.sigmoid(a_mla + b_gate[:D_MODEL])
    gate_w = jax.nn.sigmoid(a_swa + b_gate[D_MODEL:])
    merged = gate_m * (o_m @ w_br_mla) + gate_w * (o_w @ w_br_swa)
    return x + merged @ w_out

def moe_ffn(x, g_moe, w_router, router_bias, w_exp_gu, w_exp_down, w_sh_gu, w_sh_down):
    B, S, D = x.shape
    h = rmsnorm(x, g_moe).reshape(B * S, D)
    T = h.shape[0]
    scores = jax.nn.sigmoid((h @ w_router).astype(jnp.float32))
    sel = scores + router_bias.astype(jnp.float32)
    grp = sel.reshape(T, N_GROUPS, EXPERTS_PER_GROUP)
    gscore = jnp.sum(lax.top_k(grp, 2)[0], axis=-1)
    _, gidx = lax.top_k(gscore, TOPK_GROUPS)
    gmask = jnp.sum(jax.nn.one_hot(gidx, N_GROUPS, dtype=jnp.float32), axis=-2) > 0
    emask = jnp.repeat(gmask, EXPERTS_PER_GROUP, axis=-1)
    _, eidx = lax.top_k(jnp.where(emask, sel, NEG_INF), TOP_K)
    w = jnp.take_along_axis(scores, eidx, axis=-1)
    w = w / jnp.sum(w, axis=-1, keepdims=True) * ROUTED_SCALE
    combine = jnp.einsum('tk,tke->te', w, jax.nn.one_hot(eidx, N_EXPERTS, dtype=jnp.float32)).astype(h.dtype)

    xc = h.reshape(T // MOE_CHUNK, MOE_CHUNK, D)
    cc = combine.reshape(T // MOE_CHUNK, MOE_CHUNK, N_EXPERTS)

    def chunk(args):
        xt, ct = args
        gu = jnp.einsum('td,edf->tef', xt, w_exp_gu)
        g, u = jnp.split(gu, 2, axis=-1)
        hid = jax.nn.silu(g) * u * ct[..., None]
        return jnp.einsum('tef,efd->td', hid, w_exp_down)

    routed = lax.map(chunk, (xc, cc)).reshape(T, D)
    sg, su = jnp.split(h @ w_sh_gu, 2, axis=-1)
    shared = (jax.nn.silu(sg) * su) @ w_sh_down
    return x + (routed + shared).reshape(B, S, D)

def per_layer_embedding(x, p_i, g_ple, w_ple_gate, b_ple, w_ple_proj):
    gate = jax.nn.sigmoid(rmsnorm(x, g_ple) @ w_ple_gate + b_ple)
    return x + gate * (p_i @ w_ple_proj)

def setup_inputs(seed: int = 0) -> dict:
    key = jax.random.key(seed)
    ks = iter(jax.random.split(key, 40))
    L = DEPTH

    def dense(shape, fan_in):
        return jax.random.normal(next(ks), shape, jnp.float32) * (fan_in ** -0.5)

    def gain(n):
        return 1.0 + 0.05 * jax.random.normal(next(ks), (L, n), jnp.float32)

    x = jax.random.normal(next(ks), (BATCH, SEQ, D_MODEL), jnp.float32)
    p = jax.random.normal(next(ks), (DEPTH, BATCH, SEQ, PLE_DIM), jnp.float32)
    offset = jax.random.randint(next(ks), (BATCH, 1), 0, 1024, dtype=jnp.int32)
    positions = offset + jnp.arange(SEQ, dtype=jnp.int32)[None, :]
    return {
        "x": x,
        "p": p,
        "positions": positions,
        "g_mix": gain(D_MODEL),
        "w_in": dense((L, D_MODEL, IN_WIDTH), D_MODEL),
        "b_gate": 0.1 * jax.random.normal(next(ks), (L, 2 * D_MODEL), jnp.float32),
        "g_cq": gain(MLA_Q_RANK),
        "w_uq": dense((L, MLA_Q_RANK, MLA_HEADS * MLA_QK), MLA_Q_RANK),
        "g_ckv": gain(MLA_KV_RANK),
        "w_ukv": dense((L, MLA_KV_RANK, MLA_HEADS * (MLA_NOPE + MLA_V)), MLA_KV_RANK),
        "g_qn_mla": gain(MLA_QK),
        "g_kn_mla": gain(MLA_QK),
        "g_qn_swa": gain(SWA_HD),
        "g_kn_swa": gain(SWA_HD),
        "sink": 0.5 * jax.random.normal(next(ks), (L, SWA_HEADS), jnp.float32),
        "w_br_mla": dense((L, MLA_HEADS * MLA_V, D_MODEL), MLA_HEADS * MLA_V),
        "w_br_swa": dense((L, SWA_HEADS * SWA_HD, D_MODEL), SWA_HEADS * SWA_HD),
        "w_out": dense((L, D_MODEL, D_MODEL), D_MODEL),
        "g_moe": gain(D_MODEL),
        "w_router": dense((L, D_MODEL, N_EXPERTS), D_MODEL),
        "router_bias": 0.01 * jax.random.normal(next(ks), (L, N_EXPERTS), jnp.float32),
        "w_exp_gu": dense((L, N_EXPERTS, D_MODEL, 2 * EXPERT_FF), D_MODEL),
        "w_exp_down": dense((L, N_EXPERTS, EXPERT_FF, D_MODEL), EXPERT_FF),
        "w_sh_gu": dense((L, D_MODEL, 2 * SHARED_FF), D_MODEL),
        "w_sh_down": dense((L, SHARED_FF, D_MODEL), SHARED_FF),
        "g_ple": gain(D_MODEL),
        "w_ple_gate": dense((L, D_MODEL, D_MODEL), D_MODEL),
        "b_ple": 0.1 * jax.random.normal(next(ks), (L, D_MODEL), jnp.float32),
        "w_ple_proj": dense((L, PLE_DIM, D_MODEL), PLE_DIM),
    }

def reference(x, p, positions, g_mix, w_in, b_gate, g_cq, w_uq, g_ckv, w_ukv, g_qn_mla, g_kn_mla,
              g_qn_swa, g_kn_swa, sink, w_br_mla, w_br_swa, w_out, g_moe, w_router, router_bias,
              w_exp_gu, w_exp_down, w_sh_gu, w_sh_down, g_ple, w_ple_gate, b_ple, w_ple_proj):
    cos_s, sin_s = rope_cos_sin(positions, SWA_HD)
    cos_m, sin_m = rope_cos_sin(positions, MLA_ROPE)
    for i in range(DEPTH):
        x = token_mixers(x, cos_s, sin_s, cos_m, sin_m, g_mix[i], w_in[i], b_gate[i], g_cq[i], w_uq[i],
                         g_ckv[i], w_ukv[i], g_qn_mla[i], g_kn_mla[i], g_qn_swa[i], g_kn_swa[i], sink[i],
                         w_br_mla[i], w_br_swa[i], w_out[i])
        x = moe_ffn(x, g_moe[i], w_router[i], router_bias[i], w_exp_gu[i], w_exp_down[i],
                    w_sh_gu[i], w_sh_down[i])
        x = per_layer_embedding(x, p[i], g_ple[i], w_ple_gate[i], b_ple[i], w_ple_proj[i])
    return x


_drawn_inputs = setup_inputs


def setup_inputs(seed=0):
    import zlib

    import numpy as np

    out = dict(_drawn_inputs(seed))
    spreads = {}
    factors = {'g_qn_swa': 2.809, 'sink': 4.84, 'g_ple': 7.399, 'b_ple': 4.112, 'g_qn_mla': 3.069}
    for name, (base, spread) in spreads.items():
        noise = np.random.default_rng([zlib.crc32(name.encode()), seed]).standard_normal(out[name].shape)
        drawn = base * np.exp(spread * noise) if base else spread * noise
        out[name] = __import__('jax').numpy.asarray(drawn.astype(out[name].dtype))
    for name, factor in factors.items():
        out[name] = (out[name] * factor).astype(out[name].dtype)
    return out
```

```python
import math
from contextlib import ExitStack

import concourse.bass as bass
from concourse import mybir

P = 128
BANK = 512
T, D = 512, 1024
NT, KD = T // P, D // P
PLE = 256
EPS = 1e-6
THETA = 10000.0
NEG = -1e30

MH, Q_RANK, KV_RANK, NOPE, ROPE, VD = 8, 384, 256, 64, 32, 64
QK = NOPE + ROPE
WH, WKV, HD = 8, 2, 64
C_CKV = Q_RANK
C_KR = C_CKV + KV_RANK
C_QS = C_KR + ROPE
C_KS = C_QS + WH * HD
C_VS = C_KS + WKV * HD
C_GATE = C_VS + WKV * HD
IN_W = C_GATE + 2 * D
Z_CHUNK = C_GATE // 3
C_BLOCKS = (Q_RANK + KV_RANK) // P
Q_BLOCKS = Q_RANK // P

E, TOPK, GROUPS, TOPG = 64, 8, 8, 4
PER_GROUP = E // GROUPS
FF, SH = 256, 256
ROUTED_SCALE = 2.5
SLOTS = 96
TILES_MAX = -(-T // SLOTS)
RING = 4
NO_ROW = 32768.0
UNITS = 2 * NT * 8

ROUND = 12582912.0
TWO_PI = (201.0 / 32, 8117.0 / 2 ** 22, 2 * math.pi - 201.0 / 32 - 8117.0 / 2 ** 22)

F_M, F_S = ROPE // 2, HD // 2
NF = F_M + F_S


def build(nc, x, p, positions, g_mix, w_in, b_gate, g_cq, w_uq, g_ckv, w_ukv, g_qn_mla, g_kn_mla,
          g_qn_swa, g_kn_swa, sink, w_br_mla, w_br_swa, w_out, g_moe, w_router, router_bias,
          w_exp_gu, w_exp_down, w_sh_gu, w_sh_down, g_ple, w_ple_gate, b_ple, w_ple_proj,
          rope_freq, out):
    f32, bf16, i32, u32 = mybir.dt.float32, mybir.dt.bfloat16, mybir.dt.int32, mybir.dt.uint32
    ALU, ACT, AX = mybir.AluOpType, mybir.ActivationFunctionType, mybir.AxisListType

    with ExitStack() as ctx:
        def sb(name, shape, dt=f32):
            return ctx.enter_context(nc.sbuf_tensor(name, shape, dt))

        def sem(name):
            return ctx.enter_context(nc.semaphore(name))

        h_rows = nc.dram_tensor("h_rows", [T, D], f32).ap()
        y_rows = nc.dram_tensor("y_rows", [T * TOPK, D], f32).ap()
        pp_rows = nc.dram_tensor("pp_rows", [T, D], f32).ap()

        arena = sb("arena", [P, 50816])

        def view(at, *dims):
            n = math.prod(dims)
            v = arena[:, at:at + n]
            if len(dims) == 2:
                v = v.rearrange("p (a b) -> p a b", b=dims[1])
            if len(dims) == 3:
                v = v.rearrange("p (a b c) -> p a b c", b=dims[1], c=dims[2])
            return v

        x_sb = view(0, NT, D)
        hT = view(4096, KD, T)
        z = view(8192, NT, C_GATE)
        w_g = [view(13952 + 2048 * s, KD, 2 * P) for s in range(3)]
        w1 = view(20096, KD, C_GATE)
        q_sb = view(20096, NT, MH * QK)
        kk = view(23168, NT, MH * QK)
        kv = view(26240, NT, MH * (NOPE + VD))
        gT = view(31616, 2 * KD, T)
        cT = view(39808, C_BLOCKS, T)
        wuq = view(42368, Q_BLOCKS, MH * QK)
        wukv = view(44672, KV_RANK // P, MH * (NOPE + VD))
        xn = view(46720, 2, D)
        g_mix_b = view(48768, D)
        sq = view(46720, 1952)
        rope_t = view(48672, 4, 320)
        g_cq_b = view(49952, Q_RANK)
        g_ckv_b = view(50336, KV_RANK)
        c_n = view(48672, 2, C_BLOCKS * P)
        ang = view(48672, 6, NT * NF)
        p_sb = view(31616, NT, PLE)
        pT = view(32640, PLE // P, T)
        w_pp = view(33664, PLE // P, D)
        pp_st = view(35712, 2, D)
        qT = view(4096, MH, T)
        kT = view(13952, MH, T)
        prob = view(18048, 2, T)
        probT = view(19072, 2, NT * P)
        qwT = view(39808, WH // 2, T)
        k_dup = view(41856, NT, 2 * WKV * HD)
        kwT = view(42880, WKV, T)
        oT_w = view(43904, NT, T)
        o_sb = view(45952, MH * VD)
        oT_m = view(24192, NT, T)
        w_bm = view(20096, MH * VD // P, D)
        w_bs = view(46720, WH * HD // P, D)
        mT = view(4096, KD, T)
        w_o = view(8192, KD, D)
        br_t = view(45952, T)
        g_moe_b = view(16384, D)
        h2 = view(17408, 2, D)
        junk2 = view(19456, D)
        h2T = view(31616, KD, T)
        w_sg = view(26240, KD, 2 * SH)
        w_sd = view(35712, SH // P, D)
        w_r = view(37760, KD, E)
        shT = view(38272, SH // P, T)
        rt = [view(46720 + 256 * i, NT, E) for i in range(8)]
        info = arena[:, 48768:49792].bitcast(bf16).rearrange("p (e a c) -> p e a c", a=NT, c=8)
        grp = view(49792, 4, 256)
        w_gu = [view(4096 * (1 + s), KD, 2 * FF) for s in range(RING)]
        w_dn = [view(20480 + 2048 * s, FF // P, D) for s in range(RING)]
        w_pg = view(28672, KD, D)
        g_ple_b = view(36864, D)
        b_ple_b = view(37888, D)
        iota = view(38912, TILES_MAX * SLOTS)
        iot_i = arena[:, 39808:39808 + TILES_MAX * SLOTS].bitcast(i32)
        rank = view(39488, NT, E)
        xg = view(39808, 2, D)
        xT = view(41856, 2, KD, SLOTS)
        hidT = view(43392, 2, FF // P, SLOTS)
        sg = view(43776, 2, FF // P, SLOTS)
        y_sb = view(44160, 2, D)
        onehot = arena[:, 46208:46592].bitcast(bf16).rearrange("p (r a s) -> p r a s", r=2, a=NT)
        y_in = [view(4096 + 8192 * b, TOPK, D) for b in range(2)]
        h3 = view(20480, 2, D)
        h3T = view(22528, 2, KD, P)
        gate3 = view(24576, 2, D)
        out_st = view(26624, 2, D)
        pp_in = view(46720, 2, D)
        junk3 = view(39808, D)

        ident = sb("ident", [P, P])
        ident_b = sb("ident_b", [P, P], bf16)
        before_b = sb("before_b", [P, P], bf16)
        ones_b = sb("ones_b", [P, P], bf16)
        band_b = sb("band_b", [P, 2, P], bf16)
        rows = sb("rows", [2 * KD, P])
        pos_f = sb("pos_f", [NT, P])
        pos_i = sb("pos_i", [NT, P], i32)
        cols = sb("cols", [P, 2 * KD + NT])
        freq = sb("freq", [P, NF])
        cs = sb("cs", [P, 2, NT, NF])
        g_q = sb("g_q", [P, QK])
        g_k = sb("g_k", [P, QK])
        g_s = sb("g_s", [P, 2, HD])
        sink_b = sb("sink_b", [P, WH])
        ssum = sb("ssum", [P, 32])
        rs = sb("rs", [P, 32])
        half = sb("half", [P, 32])
        nmax = sb("nmax", [P, UNITS])
        lsum = sb("lsum", [P, UNITS])
        es = sb("es", [P, 2 * WH])
        wj = sb("wj", [P, NT, TOPK])
        idx = sb("idx", [SLOTS, RING, 2], u32)
        idx_f = sb("idx_f", [SLOTS, 2, 2])
        info_t = sb("info_t", [P, 2, NT * 8], bf16)
        more = sb("more", [E, 4 * 8])
        more_b = sb("more_b", [E, 2], bf16)
        table = sb("table", [1, 3, E], i32)
        rtmp = sb("rtmp", [P, 32])
        mx1 = sb("mx1", [P, 2])
        tcol = sb("tcol", [P, 2])
        mask_b = sb("mask_b", [P, NT, E], bf16)
        kr_t = view(50592, 6, F_M)
        bank = [ctx.enter_context(nc.psum_tensor(f"bank{b}", [P, BANK], f32)) for b in range(8)]

        d_small, d_p, d_wu, d_bm, d_bs, d_wo, d_sg, d_sd, d_wr, d_ple = [
            sem(n) for n in ("d_small", "d_p", "d_wu", "d_bm", "d_bs", "d_wo", "d_sg", "d_sd", "d_wr", "d_ple")]
        d_x = [sem(f"d_x{t}") for t in range(NT)]
        d_w1 = [sem(f"d_w1_{k}") for k in range(KD)]
        d_wg = [sem(f"d_wg{s}") for s in range(3)]
        d_pps = [sem(f"d_pps{s}") for s in range(2)]
        d_h2 = [sem(f"d_h2_{s}") for s in range(2)]
        d_gu = [sem(f"d_gu{s}") for s in range(RING)]
        d_dn = [sem(f"d_dn{s}") for s in range(RING)]
        d_xg = [sem(f"d_xg{s}") for s in range(2)]
        d_sc = [sem(f"d_sc{s}") for s in range(2)]
        d_y = [sem(f"d_y{s}") for s in range(2)]
        d_ppi = [sem(f"d_ppi{s}") for s in range(2)]
        d_out = [sem(f"d_out{s}") for s in range(2)]
        (pe_rows, pe_pT, pe_pp, pe_hT, pe_z, pe_cT, pe_up, pe_g, pe_tr, pe_s, pe_t, pe_pv, pe_ot, pe_br, pe_wo,
         pe_h2T, pe_lg, pe_sh, pe_sd, pe_rank, pe_cnt, pe_st, pe_tab, pe_info, pe_T, pe_gu, pe_dn, pe_h3T,
         pe_pg) = [sem("pe_" + n) for n in (
             "rows pT pp hT z cT up g tr s t pv ot br wo h2T lg sh sd rank cnt st tab info T gu dn h3T pg").split()]
        (a_pT, a_ss, a_pp, a_hT, a_z, a_c, a_cT, a_up, a_g, a_sq, a_trig, a_tr, a_e, a_pt, a_es, a_oT, a_ss2, a_h2T,
         a_sc, a_ssh, a_xT, a_sg, a_y, a_ss3, a_h3T, a_gate) = [sem("a_" + n) for n in (
             "pT ss pp hT z c cT up g sq trig tr e pt es oT ss2 h2T sc ssh xT sg y ss3 h3T gate").split()]
        (v_cols, v_xn, v_pp, v_hT, v_z, v_cn, v_cT, v_up, v_trig, v_red, v_nrm, v_tr, v_nm, v_pt, v_es, v_o, v_br,
         v_mT, v_x1, v_h2, v_h2T, v_sh, v_base, v_mask, v_rank, v_more, v_hot, v_tab, v_idx, v_xT, v_hid, v_y,
         v_comb, v_h3, v_h3T, v_gb, v_step, v_idf, v_oh) = [sem("v_" + n) for n in (
             "cols xn pp hT z cn cT up trig red nrm tr nm pt es o br mT x1 h2 h2T sh base mask rank more hot tab "
             "idx xT hid y comb h3 h3T gb step idf oh").split()]
        (p_const, p_pos, p_rs, p_rsc, p_rsq, p_prep, p_rs2, p_iota, p_routed, p_rs3, p_out, p_step) = [
            sem("p_" + n) for n in "const pos rs rsc rsq prep rs2 iota routed rs3 out step".split()]
        N_SMALL = 11

        block = ctx.enter_context(nc.Block())

        def linker(eng, step_sem):
            count = [0]

            def link(ins):
                count[0] += 1
                ins.then_inc(step_sem, 1)
                eng.wait_ge(step_sem, count[0])
            return link

        def tsl(t):
            return slice(t * P, (t + 1) * P)

        units = [(qt, kind, h) for qt in range(NT) for kind in (0, 1) for h in range(8)]

        def band(qt):
            lo, hi = max(0, qt - 1), min(NT - 1, qt + 1)
            return lo, hi - lo + 1

        class Item:
            def __init__(self, n, s, uses4, uses2, over=False):
                self.n, self.s4, self.s2 = n, s, s % 2
                self.uses4, self.uses2 = uses4, uses2
                self.lag2 = 1 if over else 2
                self.lag4 = 1 if over else RING
                self.sc_before = 1 if over else 2

        def item(it, s):
            return Item(RING * it + s, s, it + 1, (RING // 2) * it + s // 2 + 1)

        def over_item(j):
            return Item(E + j, 0, E // RING + 1 + j, E // 2 + 1 + j, over=True)

        def item_loop(eng, step, first, last):
            lo, hi = -(-first // RING), last // RING
            for n in range(first, min(lo * RING, last)):
                step(item(n // RING, n % RING))
            if hi > lo:
                with eng.Fori(lo, hi) as it:
                    for s in range(RING):
                        step(item(it, s))
            for n in range(max(hi * RING, first), last):
                step(item(n // RING, n % RING))

        def overflow_loop(eng, step):
            eng.wait_ge(v_tab, 3)
            count = eng.value_load(table[0:1, 2, 0:1], min_val=0, max_val=E - 1)
            with eng.If(count > 0):
                with eng.Fori(0, count) as j:
                    step(over_item(j), j)
            eng.end_ifs()

        def tail_out(pool, link, t):
            pool.wait_ge(a_gate, t + 1)
            pool.wait_ge(d_ppi[t % 2], 16 * (t // 2 + 1))
            if t >= 2:
                pool.wait_ge(d_out[t % 2], 16 * (t // 2))
            link(pool.tensor_tensor(out_st[:, t % 2], gate3[:, t % 2], pp_in[:, t % 2], ALU.mult))
            pool.tensor_tensor(out_st[:, t % 2], out_st[:, t % 2], x_sb[:, t], ALU.add).then_inc(p_out, 1)

        def tail_gate(act, t):
            act.wait_ge(v_gb, t + 1)
            act.activation(gate3[:, t % 2], gate3[:, t % 2], ACT.Sigmoid).then_inc(a_gate, 1)

        def h2T_out(act, t):
            act.wait_ge(pe_h2T, 2 * t + 1)
            act.activation(h2T[:, 0:4, tsl(t)], bank[2 * (t % 2)][:].rearrange("p (c q) -> p c q", q=P),
                           ACT.Copy).then_inc(a_h2T, 1)

        def head_out(eng, j):
            eng.wait_ge(pe_tr, j + 1)
            src = bank[j % 4]
            if j < 8:
                dst, src = qT[0:QK, j], src[0:QK, :]
            elif j < 16:
                dst, src = kT[0:QK, j - 8], src[0:QK, :]
            elif j < 20:
                dst, src = qwT[:, j - 16], src[:, :]
            else:
                dst, src = kwT[:, j - 20], src[:, :]
            if j % 2 == 0:
                eng.activation(dst, src, ACT.Copy).then_inc(a_tr, 1)
            else:
                eng.tensor_copy(dst, src).then_inc(v_tr, 1)

        def probT_out(eng, u):
            qt, kind, h = units[u]
            n = T if kind == 0 else band(qt)[1] * P
            eng.wait_ge(pe_t, u + 1)
            if u >= 2:
                eng.wait_ge(pe_pv, u - 1)
            if u % 2 == 0:
                eng.activation(probT[:, 0, 0:n], bank[3][:, 0:n], ACT.Copy).then_inc(a_pt, 1)
            else:
                eng.tensor_copy(probT[:, 1, 0:n], bank[4][:, 0:n]).then_inc(v_pt, 1)

        def pipeline(eng, xT_out, mid, y_out):
            def step(it, s):
                known, n = isinstance(it, int), RING * it + s
                if not known or n >= 2:
                    y_out(item(it + (s - 2) // RING, (s - 2) % RING))
                mid(item(it, s))
                if not known or n + 1 < E:
                    xT_out(item(it + (s + 1) // RING, (s + 1) % RING))
            xT_out(item(0, 0))
            for s in range(RING):
                step(0, s)
            with eng.Fori(1, E // RING - 1) as it:
                for s in range(RING):
                    step(it, s)
            for s in range(RING):
                step(E // RING - 1, s)
            for n in (E - 2, E - 1):
                y_out(item(n // RING, n % RING))

        def tail_bias(dve, t):
            dve.wait_ge(pe_pg, t + 1)
            if t >= 2:
                dve.wait_ge(p_out, t - 1)
            for hf in range(2):
                sl = slice(hf * BANK, (hf + 1) * BANK)
                ins = dve.tensor_tensor(gate3[:, t % 2, sl], bank[4 + 2 * (t % 2) + hf][:], b_ple_b[:, sl], ALU.add)
            ins.then_inc(v_gb, 1)

        def shift(i, d):
            if isinstance(i.n, int):
                n = i.n + d
                return item(n // RING, n % RING) if n < E else None
            it = i.uses4 - 1
            return item(it + (i.s4 + d) // RING, (i.s4 + d) % RING)

        @block.sync
        def _(sp):
            sp.dma_start(p_sb, p[0, 0].rearrange("(t p) d -> p t d", p=P)).then_inc(d_p, 16)
            sp.dma_start(w_pp, w_ple_proj[0].rearrange("(k p) d -> p k d", p=P)).then_inc(d_p, 16)
            for t in range(NT):
                sp.dma_start(x_sb[:, t], x[0, tsl(t)]).then_inc(d_x[t], 16)
            for k in range(KD):
                sp.dma_start(w1[:, k], w_in[0, tsl(k), 0:C_GATE]).then_inc(d_w1[k], 16)
            sp.dma_start(wuq, w_uq[0].rearrange("(k p) d -> p k d", p=P)).then_inc(d_wu, 16)
            sp.dma_start(wukv, w_ukv[0].rearrange("(k p) d -> p k d", p=P)).then_inc(d_wu, 16)
            for g in range(KD):
                if g >= 3:
                    sp.wait_ge(pe_g, 2 * (g - 3) + 2)
                c0 = C_GATE + g * 2 * P
                sp.dma_start(w_g[g % 3], w_in[0, :, c0:c0 + 2 * P].rearrange("(k p) c -> p k c", p=P)).then_inc(d_wg[g % 3], 16)
            sp.wait_ge(pe_tr, 2 * MH)
            sp.dma_start(w_bm, w_br_mla[0].rearrange("(k p) d -> p k d", p=P)).then_inc(d_bm, 16)
            sp.wait_ge(p_prep, NT)
            sp.dma_start(w_bs, w_br_swa[0].rearrange("(k p) d -> p k d", p=P)).then_inc(d_bs, 16)
            sp.wait_ge(pe_pv, UNITS)
            sp.dma_start(w_o, w_out[0].rearrange("(k p) d -> p k d", p=P)).then_inc(d_wo, 16)
            sp.dma_start(g_moe_b, g_moe[0].partition_broadcast(P)).then_inc(d_wr, 16)
            sp.dma_start(w_sg, w_sh_gu[0].rearrange("(k p) d -> p k d", p=P)).then_inc(d_sg, 16)
            sp.wait_ge(v_mT, KD)
            sp.dma_start(w_r, w_router[0].rearrange("(k p) d -> p k d", p=P)).then_inc(d_wr, 16)
            sp.dma_start(grp[:, 3, 0:E], router_bias[0].partition_broadcast(P)).then_inc(d_wr, 16)
            sp.dma_start(w_sd, w_sh_down[0].rearrange("(k p) d -> p k d", p=P)).then_inc(d_sd, 16)

            def load_gu(i, e=None):
                e = i.n if e is None else e
                sp.dma_start(w_gu[i.s4], w_exp_gu[0, bass.ds(e, 1)].rearrange("a (k p) f -> p (a k) f", p=P)).then_inc(d_gu[i.s4], 16)

            def load_dn(i, e=None):
                e = i.n if e is None else e
                sp.dma_start(w_dn[i.s4], w_exp_down[0, bass.ds(e, 1)].rearrange("a (k p) f -> p (a k) f", p=P)).then_inc(d_dn[i.s4], 16)

            sp.wait_ge(pe_wo, NT)
            for s in range(3):
                load_gu(item(0, s))
                if s < 2:
                    load_dn(item(0, s))
            for t in range(NT):
                sp.wait_ge(v_h2, t + 1)
                sp.dma_start(h_rows[tsl(t)], h2[:, t % 2]).then_inc(d_h2[t % 2], 16)
            sp.wait_ge(pe_sh, 4)
            load_dn(item(0, 2))
            sp.wait_ge(d_h2[0], 32)
            sp.wait_ge(d_h2[1], 32)
            load_gu(item(0, 3))
            load_dn(item(0, 3))
            sp.wait_ge(pe_sd, NT)
            sp.dma_start(w_pg, w_ple_gate[0].rearrange("(k p) d -> p k d", p=P)).then_inc(d_ple, 16)
            sp.dma_start(g_ple_b, g_ple[0].partition_broadcast(P)).then_inc(d_ple, 16)
            sp.dma_start(b_ple_b, b_ple[0].partition_broadcast(P)).then_inc(d_ple, 16)
            sp.wait_ge(v_tab, 3)
            for s in range(2):
                sp.wait_ge(d_pps[s], 32)
                sp.dma_start(pp_in[:, s], pp_rows[tsl(s)]).then_inc(d_ppi[s], 16)

            def step(i):
                sp.wait_ge(pe_gu, i.n - i.lag4 + 1)
                load_gu(i)
                sp.wait_ge(pe_dn, i.n - i.lag4 + 1)
                load_dn(i)
            item_loop(sp, step, RING, E)

            def over(i, j):
                e = sp.value_load(table[0:1, 0, bass.ds(j, 1)], min_val=0, max_val=E - 1)
                sp.wait_ge(pe_dn, i.n)
                load_gu(i, e)
                load_dn(i, e)
            overflow_loop(sp, over)

            for t in range(NT):
                if t < 2:
                    sp.wait_ge(p_routed, 1)
                else:
                    sp.wait_ge(v_comb, t - 1)
                sp.dma_start(y_in[t % 2], y_rows[t * P * TOPK:(t + 1) * P * TOPK].rearrange(
                    "(p j) d -> p j d", j=TOPK)).then_inc(d_y[t % 2], 16)
                if t >= 2:
                    sp.wait_ge(p_out, t - 1)
                    sp.dma_start(pp_in[:, t % 2], pp_rows[tsl(t)]).then_inc(d_ppi[t % 2], 16)
            for t in range(NT):
                sp.wait_ge(p_out, t + 1)
                sp.dma_start(out[0, tsl(t)], out_st[:, t % 2]).then_inc(d_out[t % 2], 16)
            sp.wait_ge(d_out[0], 32)
            sp.wait_ge(d_out[1], 32)

        @block.gpsimd
        def _(pool):
            link = linker(pool, p_step)
            link(pool.memset(ident[:], 0.0))
            link(pool.affine_select(out=ident[:], in_=ident[:], compare_op=ALU.not_equal, fill=1.0, base=0,
                                    pattern=[[-1, P]], channel_multiplier=1))
            pool.tensor_copy(ident_b[:], ident[:])
            pool.memset(half[:], -0.5)
            link(pool.memset(ones_b[:], 1.0))
            pool.affine_select(out=before_b[:], in_=ones_b[:], compare_op=ALU.is_gt, fill=0.0, base=0,
                               pattern=[[1, P]], channel_multiplier=-1)
            link(pool.memset(band_b[:], 0.0))
            pool.affine_select(out=band_b[:, 0], in_=band_b[:, 0], compare_op=ALU.is_ge, fill=NEG, base=0,
                               pattern=[[1, P]], channel_multiplier=-1)
            link(pool.affine_select(out=band_b[:, 1], in_=band_b[:, 1], compare_op=ALU.is_ge, fill=NEG, base=0,
                                    pattern=[[-1, P]], channel_multiplier=1))
            pool.wait_ge(d_small, 16 * N_SMALL)
            pool.tensor_copy(pos_f[:], pos_i[:]).then_inc(p_pos, 1)

            def rms(dst, src, n, tmp):
                link(pool.tensor_scalar(tmp, src, 1.0 / n, EPS, ALU.mult, ALU.add))
                return pool.tensor_tensor(dst, tmp, half[:, 0:tmp.shape[1]], ALU.pow)

            for t in range(NT):
                pool.wait_ge(a_ss, t + 1)
                rms(rs[:, t:t + 1], ssum[:, t:t + 1], D, rtmp[:, t:t + 1]).then_inc(p_rs, 1)
            for t in range(NT):
                pool.wait_ge(a_c, t + 1)
                link(rms(rs[:, 8 + 2 * t:9 + 2 * t], ssum[:, 8 + 2 * t:9 + 2 * t], Q_RANK, rtmp[:, 8 + 2 * t:9 + 2 * t]))
                rms(rs[:, 9 + 2 * t:10 + 2 * t], ssum[:, 9 + 2 * t:10 + 2 * t], KV_RANK, rtmp[:, 9 + 2 * t:10 + 2 * t]).then_inc(p_rsc, 1)

            pool.wait_ge(a_trig, 2)
            pool.wait_ge(v_cn, NT)
            pool.wait_ge(pe_up, NT)
            pool.wait_ge(p_rsc, NT)
            n_heads = WH + WKV
            for t in range(NT):
                pool.wait_ge(v_red, t + 1)
                if t:
                    pool.wait_ge(p_prep, t)
                link(rms(rs[:, 0:16], ssum[:, 0:16], QK, rtmp[:, 0:16]))
                link(rms(rs[:, 16:26], ssum[:, 16:26], HD, rtmp[:, 16:26]))
                link(pool.tensor_scalar(rs[:, 0:8], rs[:, 0:8], QK ** -0.5, None, ALU.mult))
                pool.tensor_scalar(rs[:, 16:24], rs[:, 16:24], HD ** -0.5, None, ALU.mult).then_inc(p_rsq, 1)
                pool.wait_ge(v_nrm, t + 1)
                pool.wait_ge(p_rsq, t + 1)
                qh = q_sb[:, t].rearrange("p (h d) -> p h d", d=QK)
                kh = kk[:, t].rearrange("p (h d) -> p h d", d=QK)
                wh = z[:, t, C_QS:C_VS].rearrange("p (h d) -> p h d", d=HD)
                link(pool.tensor_tensor(qh, qh, g_q[:, 0:QK].unsqueeze(1).broadcast_to([P, MH, QK]), ALU.mult))
                pool.tensor_tensor(kh[:, :, 0:NOPE], kh[:, :, 0:NOPE],
                                   g_k[:, 0:NOPE].unsqueeze(1).broadcast_to([P, MH, NOPE]), ALU.mult)
                pool.tensor_tensor(wh[:, 0:WH], wh[:, 0:WH], g_s[:, 0].unsqueeze(1).broadcast_to([P, WH, HD]), ALU.mult)
                link(pool.tensor_tensor(wh[:, WH:], wh[:, WH:], g_s[:, 1].unsqueeze(1).broadcast_to([P, WKV, HD]), ALU.mult))

                def rotate(v, heads, nf, f0):
                    x1, x2 = v[:, :, 0:nf], v[:, :, nf:2 * nf]
                    cos = cs[:, 0, t, f0:f0 + nf].unsqueeze(1).broadcast_to([P, heads, nf])
                    sin = cs[:, 1, t, f0:f0 + nf].unsqueeze(1).broadcast_to([P, heads, nf])
                    tmp = [rope_t[:, i, 0:heads * nf].rearrange("p (h d) -> p h d", d=nf) for i in range(4)]
                    pool.tensor_tensor(tmp[0], x1, cos, ALU.mult)
                    pool.tensor_tensor(tmp[1], x2, sin, ALU.mult)
                    pool.tensor_tensor(tmp[2], x2, cos, ALU.mult)
                    link(pool.tensor_tensor(tmp[3], x1, sin, ALU.mult))
                    pool.tensor_tensor(x1, tmp[0], tmp[1], ALU.subtract)
                    link(pool.tensor_tensor(x2, tmp[2], tmp[3], ALU.add))
                rotate(qh[:, :, NOPE:QK], MH, F_M, 0)
                rotate(wh, n_heads, F_S, F_M)
                kd = k_dup[:, t].rearrange("p (g c d) -> p g c d", c=2, d=HD)
                pool.tensor_copy(kd[:, :, 0], wh[:, WH:])
                pool.tensor_copy(kd[:, :, 1], wh[:, WH:]).then_inc(p_prep, 1)

            pool.wait_ge(p_prep, NT)
            for t in range(NT):
                pool.wait_ge(a_ss2, t + 1)
                rms(rs[:, t:t + 1], ssum[:, t:t + 1], D, rtmp[:, t:t + 1]).then_inc(p_rs2, 1)

            pool.wait_ge(v_mT, KD)
            iv = info.rearrange("p e a c -> p c a e")
            link(pool.iota(iot_i[:], pattern=[[1, TILES_MAX * SLOTS]], base=0, channel_multiplier=0))
            pool.wait_ge(pe_sd, NT)
            link(pool.tensor_copy(iota, iot_i[:]))
            link(pool.iota(iot_i[:, 0:2], pattern=[[0, 2]], base=0, channel_multiplier=1))
            link(pool.tensor_copy(tcol[:, 0:1], iot_i[:, 0:1]))
            link(pool.tensor_scalar(tcol[:, 1:2], tcol[:, 0:1], float(TOPK), None, ALU.mult))
            link(pool.memset(info, 0.0))
            pool.tensor_copy(iv[:, 0], tcol[:, 0:1].unsqueeze(2).broadcast_to([P, NT, E]))
            pool.tensor_copy(iv[:, 4], tcol[:, 1:2].unsqueeze(2).broadcast_to([P, NT, E]))
            for a in range(NT):
                pool.memset(iv[:, 1, a], float(P * a))
                pool.memset(iv[:, 5, a], float(TOPK * P * a))
            pool.memset(iv[:, 3], -NO_ROW)
            pool.memset(iv[:, 7], -NO_ROW)
            pool.memset(xg, 0.0).then_inc(p_iota, 1)

            last_h, last_y = pool.to_reg(T - 1), pool.to_reg(T * TOPK - 1)

            def held(n):
                return n if isinstance(n, int) else pool.to_reg(n)

            def gather(i):
                first = isinstance(i.n, int) and i.n < 2
                index_due = held(i.n + 1)
                turn_due = None if first else held(i.n - i.lag2 + 1)
                pool.wait_ge(p_iota, 1)
                pool.wait_ge(v_idx, index_due)
                if not first:
                    pool.wait_ge(pe_T, turn_due)
                pool.indirect_dma_start(xg[0:SLOTS, i.s2], None, h_rows, bass.IndirectOffsetOnAxis(idx[:, i.s4, 0:1], 0),
                                        bounds_check=last_h, oob_is_err=False).then_inc(d_xg[i.s2], 16)

            def scatter(i):
                y_due = held(i.n + 1)
                pool.wait_ge(p_iota, 1)
                pool.wait_ge(a_y, y_due)
                pool.wait_ge(v_y, y_due)
                pool.indirect_dma_start(y_rows, bass.IndirectOffsetOnAxis(idx[:, i.s4, 1:2], 0), y_sb[0:SLOTS, i.s2], None,
                                        bounds_check=last_y, oob_is_err=False).then_inc(d_sc[i.s2], 16)

            def at(n):
                return item(n // RING, n % RING)
            pool.wait_ge(d_h2[0], 32)
            pool.wait_ge(d_h2[1], 32)
            gather(at(0))
            gather(at(1))

            def step(it, s):
                n = RING * it + s
                def later(d):
                    return item(it + (s + d) // RING, (s + d) % RING)
                known = isinstance(it, int)
                if not known or n >= 2:
                    scatter(later(-2))
                if not known or n + 2 < E:
                    gather(later(2))
            for s in range(RING):
                step(0, s)
            with pool.Fori(1, E // RING - 1) as it:
                for s in range(RING):
                    step(it, s)
            for s in range(RING):
                step(E // RING - 1, s)
            scatter(at(E - 2))
            scatter(at(E - 1))
            pool.wait_ge(d_sc[0], 16 * (E // 2))
            pool.wait_ge(d_sc[1], 16 * (E // 2))

            def over(i, j):
                gather(i)
                scatter(i)
                pool.wait_ge(d_sc[0], 16 * i.uses2)
            overflow_loop(pool, over)
            pool.memset(half[:], -0.5).then_inc(p_routed, 1)

            pool.wait_ge(p_routed, 1)
            for t in range(NT):
                pool.wait_ge(a_ss3, t + 1)
                rms(rs[:, t:t + 1], ssum[:, t:t + 1], D, rtmp[:, t:t + 1]).then_inc(p_rs3, 1)
                if t >= 1:
                    tail_out(pool, link, t - 1)
            tail_out(pool, link, NT - 1)

        @block.scalar
        def _(act):
            act.dma_start(pos_i[:], positions[0].rearrange("(t p) -> t p", p=P)).then_inc(d_small, 16)
            act.dma_start(rows[:], b_gate[0].rearrange("(t p) -> t p", p=P)).then_inc(d_small, 16)
            act.dma_start(g_mix_b, g_mix[0].partition_broadcast(P)).then_inc(d_small, 16)
            for dst, src in ((g_cq_b, g_cq), (g_ckv_b, g_ckv), (g_q[:], g_qn_mla), (g_k[:], g_kn_mla),
                             (g_s[:, 0], g_qn_swa), (g_s[:, 1], g_kn_swa), (sink_b[:], sink), (freq[:], rope_freq)):
                act.dma_start(dst, src[0].partition_broadcast(P)).then_inc(d_small, 16)

            for t in range(NT):
                act.wait_ge(pe_pT, t + 1)
                act.activation(pT[:, :, tsl(t)], bank[4 + t][:, 0:2 * P].rearrange("p (c q) -> p c q", q=P),
                               ACT.Copy).then_inc(a_pT, 1)
            for t in range(NT):
                act.wait_ge(d_x[t], 16)
                if t:
                    act.wait_ge(a_ss, t)
                act.activation(z[:, 0, 0:D], x_sb[:, t], ACT.Square, accum_out=ssum[:, t:t + 1]).then_inc(a_ss, 1)
            for t in range(NT):
                act.wait_ge(pe_pp, t + 1)
                if t >= 2:
                    act.wait_ge(d_pps[t % 2], 16)
                act.activation(pp_st[:, t % 2, 0:BANK], bank[2 * (t % 2)][:], ACT.Copy).then_inc(a_pp, 1)
                act.wait_ge(a_pp, t + 1)
                act.wait_ge(v_pp, t + 1)
                act.dma_start(pp_rows[tsl(t)], pp_st[:, t % 2]).then_inc(d_pps[t % 2], 16)
            for t in range(NT):
                act.wait_ge(pe_hT, 2 * t + 1)
                act.activation(hT[:, 0:4, tsl(t)], bank[4 + 2 * (t % 2)][:].rearrange("p (c q) -> p c q", q=P),
                               ACT.Copy).then_inc(a_hT, 1)

            def z_out(t):
                act.wait_ge(pe_z, t + 1)
                for c in (0, 2):
                    ins = act.activation(z[:, t, c * Z_CHUNK:(c + 1) * Z_CHUNK], bank[3 * (t % 2) + c][:, 0:Z_CHUNK], ACT.Copy)
                    ins.then_inc(a_z, 1)
                act.wait_ge(a_z, 2 * t + 2)
                act.wait_ge(v_z, t + 1)
                if t:
                    act.wait_ge(a_c, t)
                act.activation(sq[:, 0:Q_RANK], z[:, t, 0:Q_RANK], ACT.Square, accum_out=ssum[:, 8 + 2 * t:9 + 2 * t])
                act.activation(sq[:, Q_RANK:C_KR], z[:, t, Q_RANK:C_KR], ACT.Square,
                               accum_out=ssum[:, 9 + 2 * t:10 + 2 * t]).then_inc(a_c, 1)

            def cT_out(t):
                act.wait_ge(pe_cT, t + 1)
                act.activation(cT[:, 0:4, tsl(t)], bank[6][:].rearrange("p (c q) -> p c q", q=P), ACT.Copy).then_inc(a_cT, 1)

            def up_out(t):
                act.wait_ge(pe_up, t + 1)
                half_q, half_kv = MH * QK // 2, MH * (NOPE + VD) // 2
                act.activation(q_sb[:, t, 0:half_q], bank[0][:, 0:half_q], ACT.Copy).then_inc(a_up, 1)
                act.activation(kv[:, t, 0:half_kv], bank[2][:], ACT.Copy).then_inc(a_up, 1)

            def gate_out(c):
                act.wait_ge(pe_g, c + 1)
                act.activation(gT[:, c], bank[4 + c % 2][:], ACT.Sigmoid, bias=cols[:, c:c + 1]).then_inc(a_g, 1)

            def squares(t):
                act.wait_ge(a_up, 2 * t + 2)
                act.wait_ge(v_up, 2 * t + 2)
                act.wait_ge(a_c, NT)
                if t:
                    act.wait_ge(v_red, t)
                act.activation(sq[:, 0:768], q_sb[:, t], ACT.Square)
                act.activation(sq[:, 768:1280].rearrange("p (h d) -> p h d", d=NOPE),
                               kv[:, t].rearrange("p (h d) -> p h d", d=NOPE + VD)[:, :, 0:NOPE], ACT.Square)
                act.activation(sq[:, 1280:1952], z[:, t, C_KR:C_VS], ACT.Square).then_inc(a_sq, 1)

            z_out(0); z_out(1); cT_out(0); z_out(2); cT_out(1); z_out(3); cT_out(2)
            act.wait_ge(v_cols, 1)
            act.wait_ge(d_pps[0], 32)
            act.wait_ge(d_pps[1], 32)
            gate_out(0)
            cT_out(3)
            for t in range(NT):
                up_out(t)
                gate_out(t + 1) if t < 3 else None
            for c in (0, 1):
                act.wait_ge(v_trig, 1)
                act.activation(cs[:, 1 - c].rearrange("p t f -> p (t f)"), ang[:, 4 + c], ACT.Sin).then_inc(a_trig, 1)
            for t in range(NT):
                squares(t)
                for c in range(4 + 3 * t, 7 + 3 * t):
                    gate_out(c)

            for j in range(0, 22, 2):
                head_out(act, j)

            act.wait_ge(d_small, 16 * N_SMALL)
            last = UNITS - 1
            for i in range(UNITS + 16):
                if i < UNITS:
                    qt, kind, h = units[i]
                    n = T if kind == 0 else band(qt)[1] * P
                    act.wait_ge(v_nm, i + 1)
                    act.wait_ge(pe_s, i + 1)
                    if i >= 2:
                        act.wait_ge(pe_t, i - 1)
                    act.activation(prob[:, i % 2, 0:n], bank[i % 3][:, 0:n], ACT.Exp, bias=nmax[:, i:i + 1],
                                   accum_out=lsum[:, i:i + 1]).then_inc(a_e, 1)
                if 0 <= i - 2 < UNITS and i % 2 == 0:
                    probT_out(act, i - 2)
                if i >= 10 and (i - 10) % 16 == 8:
                    g = (i - 10) // 8
                    act.wait_ge(v_es, (g + 1) // 2)
                    act.activation(es[:, 0:WH], es[:, WH:2 * WH], ACT.Exp).then_inc(a_es, 1)
                if i >= 13 and (i - 13) % 8 == 0 and (i - 13) // 8 < 2 * NT:
                    g = (i - 13) // 8
                    act.wait_ge(pe_ot, g + 1)
                    dst = (oT_m, oT_w)[g % 2]
                    act.activation(dst[:, :, tsl(g // 2)], bank[7][:].rearrange("p (c q) -> p c q", q=P),
                                   ACT.Copy).then_inc(a_oT, 1)

            for t in range(NT):
                act.wait_ge(v_x1, 2 * t + 2)
                if t:
                    act.wait_ge(a_ss2, t)
                act.activation(junk2, x_sb[:, t], ACT.Square, accum_out=ssum[:, t:t + 1]).then_inc(a_ss2, 1)
                if t >= 1:
                    h2T_out(act, t - 1)
            h2T_out(act, NT - 1)
            act.wait_ge(pe_lg, 1)
            act.activation(rt[0].rearrange("p a e -> p (a e)"), bank[4][:, 0:NT * E], ACT.Sigmoid).then_inc(a_sc, 1)
            for c in range(2):
                act.wait_ge(pe_sh, c + 1)
                act.activation(shT[:, c], bank[5 + c][:], ACT.Silu).then_inc(a_ssh, 1)

            def xT_out(i):
                act.wait_ge(pe_T, i.n + 1)
                if not (isinstance(i.n, int) and i.n < 2):
                    act.wait_ge(pe_gu, i.n - i.lag2 + 1)
                act.activation(xT[:, i.s2, 0:4], bank[0][:, 0:4 * SLOTS].rearrange("p (k s) -> p k s", s=SLOTS),
                               ACT.Copy).then_inc(a_xT, 1)

            def silu(i):
                act.wait_ge(pe_gu, i.n + 1)
                if not (isinstance(i.n, int) and i.n < 2):
                    act.wait_ge(v_hid, i.n - i.lag2 + 1)
                act.activation(sg[:, i.s2], bank[2 + i.s2][:, 0:2 * SLOTS].rearrange("p (c s) -> p c s", s=SLOTS),
                               ACT.Silu).then_inc(a_sg, 1)

            def y_out(i):
                act.wait_ge(pe_dn, i.n + 1)
                if not (isinstance(i.n, int) and i.n < 2):
                    act.wait_ge(d_sc[i.s2], 16 * (i.uses2 - 1))
                act.activation(y_sb[0:SLOTS, i.s2, 0:BANK], bank[4][0:SLOTS, :], ACT.Copy).then_inc(a_y, 1)

            pipeline(act, lambda i: xT_out(i), silu, y_out)

            def over(i, j):
                xT_out(i)
                silu(i)
                y_out(i)
            overflow_loop(act, over)

            for t in range(NT):
                act.wait_ge(v_comb, t + 1)
                act.wait_ge(a_ss3, t) if t else act.wait_ge(p_routed, 1)
                act.activation(junk3, x_sb[:, t], ACT.Square, accum_out=ssum[:, t:t + 1]).then_inc(a_ss3, 1)
                act.wait_ge(pe_h3T, t + 1)
                act.activation(h3T[:, t % 2, 0:4], bank[2 * (t % 2)][:].rearrange("p (c q) -> p c q", q=P),
                               ACT.Copy).then_inc(a_h3T, 1)
                if t >= 1:
                    tail_gate(act, t - 1)
            tail_gate(act, NT - 1)

        @block.vector
        def _(dve):
            link = linker(dve, v_step)
            dve.wait_ge(pe_rows, 1)
            dve.tensor_copy(cols[:], bank[7][:, 0:2 * KD + NT]).then_inc(v_cols, 1)
            dve.wait_ge(d_small, 16 * N_SMALL)

            def xn_tile(t):
                dve.wait_ge(p_rs, t + 1)
                dve.wait_ge(d_x[t], 16)
                if t >= 2:
                    dve.wait_ge(pe_hT, 2 * (t - 2) + 2)
                dve.scalar_tensor_tensor(xn[:, t % 2], x_sb[:, t], rs[:, t:t + 1], g_mix_b, ALU.mult, ALU.mult).then_inc(v_xn, 1)

            def hT_tile(t):
                dve.wait_ge(pe_hT, 2 * t + 2)
                dve.tensor_copy(hT[:, 4:8, tsl(t)], bank[5 + 2 * (t % 2)][:].rearrange("p (c q) -> p c q", q=P)).then_inc(v_hT, 1)

            xn_tile(0); xn_tile(1)
            for t in range(NT):
                dve.wait_ge(pe_pp, t + 1)
                if t >= 2:
                    dve.wait_ge(d_pps[t % 2], 16)
                dve.tensor_copy(pp_st[:, t % 2, BANK:D], bank[2 * (t % 2) + 1][:]).then_inc(v_pp, 1)
            hT_tile(0); xn_tile(2); hT_tile(1); xn_tile(3); hT_tile(2); hT_tile(3)

            def z_tile(t):
                dve.wait_ge(pe_z, t + 1)
                dve.wait_ge(a_ss, NT)
                dve.tensor_copy(z[:, t, Z_CHUNK:2 * Z_CHUNK], bank[3 * (t % 2) + 1][:, 0:Z_CHUNK]).then_inc(v_z, 1)
                dve.wait_ge(a_z, 2 * t + 2)
                dve.wait_ge(v_z, t + 1)
                dve.wait_ge(p_rsc, t + 1)
                if t >= 2:
                    dve.wait_ge(pe_cT, t - 1)
                dve.scalar_tensor_tensor(c_n[:, t % 2, 0:Q_RANK], z[:, t, 0:Q_RANK], rs[:, 8 + 2 * t:9 + 2 * t],
                                         g_cq_b, ALU.mult, ALU.mult)
                dve.scalar_tensor_tensor(c_n[:, t % 2, Q_RANK:C_KR], z[:, t, Q_RANK:C_KR], rs[:, 9 + 2 * t:10 + 2 * t],
                                         g_ckv_b, ALU.mult, ALU.mult).then_inc(v_cn, 1)

            def cT_tile(t):
                dve.wait_ge(pe_cT, t + 1)
                dve.tensor_copy(cT[:, 4, tsl(t)], bank[7][:, 0:P]).then_inc(v_cT, 1)

            z_tile(0); z_tile(1); cT_tile(0); z_tile(2); cT_tile(1); z_tile(3); cT_tile(2); cT_tile(3)
            half_q, half_kv = MH * QK // 2, MH * (NOPE + VD) // 2
            for t in range(NT):
                dve.wait_ge(pe_up, t + 1)
                dve.tensor_copy(q_sb[:, t, half_q:], bank[1][:, 0:half_q]).then_inc(v_up, 1)
                dve.tensor_copy(kv[:, t, half_kv:], bank[3][:]).then_inc(v_up, 1)

            a, turns, r0, r1, r, rc = (ang[:, i] for i in range(6))
            for t in range(NT):
                ins = dve.tensor_scalar(a[:, t * NF:(t + 1) * NF], freq[:], cols[:, 2 * KD + t:2 * KD + t + 1], None, ALU.mult)
            link(ins)
            link(dve.tensor_scalar(turns, a, 1.0 / (2 * math.pi), ROUND, ALU.mult, ALU.add))
            link(dve.tensor_scalar(turns, turns, ROUND, None, ALU.subtract))
            link(dve.scalar_tensor_tensor(r0, turns, -TWO_PI[0], a, ALU.mult, ALU.add))
            link(dve.scalar_tensor_tensor(r1, turns, -TWO_PI[1], r0, ALU.mult, ALU.add))
            link(dve.scalar_tensor_tensor(r0, turns, -TWO_PI[2], r1, ALU.mult, ALU.add))
            link(dve.tensor_scalar(r, r0, 3.1415925, -3.1415925, ALU.min, ALU.max))
            link(dve.scalar_tensor_tensor(r1, r, -1.0, r, ALU.mult, ALU.max))
            dve.tensor_scalar(rc, r1, -1.0, math.pi / 2, ALU.mult, ALU.add).then_inc(v_trig, 1)
            dve.wait_ge(a_trig, 2)

            for t in range(NT):
                dve.wait_ge(a_sq, t + 1)
                if t:
                    dve.wait_ge(p_rsq, t)
                dve.tensor_reduce(ssum[:, 0:8], sq[:, 0:768].rearrange("p (h d) -> p h d", d=QK), AX.X, ALU.add)
                dve.tensor_reduce(ssum[:, 8:16], sq[:, 768:1280].rearrange("p (h d) -> p h d", d=NOPE), AX.X, ALU.add)
                dve.tensor_reduce(ssum[:, 26:27], sq[:, 1280:1312], AX.X, ALU.add)
                link(dve.tensor_reduce(ssum[:, 16:26], sq[:, 1312:1952].rearrange("p (h d) -> p h d", d=HD), AX.X, ALU.add))
                dve.tensor_scalar(ssum[:, 8:16], ssum[:, 8:16], ssum[:, 26:27], None, ALU.add).then_inc(v_red, 1)
                dve.wait_ge(p_rsq, t + 1)
                qh = q_sb[:, t].rearrange("p (h d) -> p h d", d=QK)
                kh = kk[:, t].rearrange("p (h d) -> p h d", d=QK)
                kvh = kv[:, t].rearrange("p (h d) -> p h d", d=NOPE + VD)
                wh = z[:, t, C_QS:C_VS].rearrange("p (h d) -> p h d", d=HD)
                dve.tensor_tensor(qh, qh, rs[:, 0:8].unsqueeze(2).broadcast_to([P, MH, QK]), ALU.mult)
                dve.tensor_tensor(kh[:, :, 0:NOPE], kvh[:, :, 0:NOPE], rs[:, 8:16].unsqueeze(2).broadcast_to([P, MH, NOPE]), ALU.mult)
                dve.tensor_tensor(wh, wh, rs[:, 16:26].unsqueeze(2).broadcast_to([P, WH + WKV, HD]), ALU.mult)
                krg = kr_t[:, 0:2]
                link(dve.tensor_tensor(krg.rearrange("p a f -> p (a f)"), z[:, t, C_KR:C_QS], g_k[:, NOPE:QK], ALU.mult))
                cos, sin = cs[:, 0, t, 0:F_M], cs[:, 1, t, 0:F_M]
                dve.tensor_tensor(kr_t[:, 2], krg[:, 0], cos, ALU.mult)
                dve.tensor_tensor(kr_t[:, 3], krg[:, 1], sin, ALU.mult)
                dve.tensor_tensor(kr_t[:, 4], krg[:, 1], cos, ALU.mult)
                link(dve.tensor_tensor(kr_t[:, 5], krg[:, 0], sin, ALU.mult))
                dve.tensor_tensor(krg[:, 0], kr_t[:, 2], kr_t[:, 3], ALU.subtract)
                link(dve.tensor_tensor(krg[:, 1], kr_t[:, 4], kr_t[:, 5], ALU.add))
                dve.tensor_tensor(kh[:, :, NOPE:QK], krg.rearrange("p a f -> p (a f)").unsqueeze(1).broadcast_to([P, MH, ROPE]),
                                  rs[:, 8:16].unsqueeze(2).broadcast_to([P, MH, ROPE]), ALU.mult).then_inc(v_nrm, 1)

            for j in range(1, 22, 2):
                head_out(dve, j)

            def group_out(g):
                qt, kind = g // 2, g % 2
                dve.wait_ge(pe_pv, 8 * g + 8)
                dve.wait_ge(a_e, 8 * g + 8)
                ls = lsum[:, 8 * g:8 * g + 8]
                if kind:
                    dve.wait_ge(a_es, qt + 1)
                    link(dve.tensor_tensor(ls, ls, es[:, 0:WH], ALU.add))
                link(dve.reciprocal(ls, ls))
                if g:
                    dve.wait_ge(pe_ot, g)
                dve.tensor_tensor(o_sb.rearrange("p (h d) -> p h d", d=VD), bank[5 + g % 2][:].rearrange("p (h d) -> p h d", d=VD),
                                  ls.unsqueeze(2).broadcast_to([P, 8, VD]), ALU.mult).then_inc(v_o, 1)

            for i in range(UNITS + 16):
                if i < UNITS:
                    qt, kind, h = units[i]
                    n = T if kind == 0 else band(qt)[1] * P
                    dve.wait_ge(pe_s, i + 1)
                    if kind == 0:
                        dve.tensor_reduce(nmax[:, i:i + 1], bank[i % 3][:, 0:n], AX.X, ALU.max, negate=True).then_inc(v_nm, 1)
                    else:
                        link(dve.tensor_reduce(mx1[:, i % 2:i % 2 + 1], bank[i % 3][:, 0:n], AX.X, ALU.max))
                        dve.tensor_scalar(nmax[:, i:i + 1], mx1[:, i % 2:i % 2 + 1], sink_b[:, h:h + 1], -1.0, ALU.max, ALU.mult).then_inc(v_nm, 1)
                if 0 <= i - 2 < UNITS and i % 2 == 1:
                    probT_out(dve, i - 2)
                if i >= 9 and (i - 9) % 16 == 8 and (i - 9) // 8 < 2 * NT:
                    g = (i - 9) // 8
                    dve.wait_ge(v_nm, 8 * g + 8)
                    if g > 1:
                        dve.wait_ge(a_es, g // 2)
                    dve.tensor_tensor(es[:, WH:2 * WH], sink_b[:], nmax[:, 8 * g:8 * g + 8], ALU.add).then_inc(v_es, 1)
                if i >= 11 and (i - 11) % 8 == 0 and (i - 11) // 8 < 2 * NT:
                    group_out((i - 11) // 8)

            for c in range(KD):
                dve.wait_ge(pe_br, c + 1)
                dve.wait_ge(a_g, 2 * KD)
                if c:
                    dve.wait_ge(v_mT, c)
                dve.tensor_tensor(mT[:, c], bank[c % 2][:], gT[:, c], ALU.mult)
                dve.tensor_tensor(br_t, bank[2 + c % 2][:], gT[:, KD + c], ALU.mult).then_inc(v_br, 1)
                dve.wait_ge(v_br, c + 1)
                dve.tensor_tensor(mT[:, c], mT[:, c], br_t, ALU.add).then_inc(v_mT, 1)
            for t in range(NT):
                dve.wait_ge(pe_wo, t + 1)
                for hf in range(2):
                    sl = slice(hf * BANK, (hf + 1) * BANK)
                    dve.tensor_tensor(x_sb[:, t, sl], bank[4 + 2 * (t % 2) + hf][:], x_sb[:, t, sl], ALU.add).then_inc(v_x1, 1)

            def h2_tile(t):
                dve.wait_ge(p_rs2, t + 1)
                dve.wait_ge(d_wr, 48)
                dve.wait_ge(v_x1, 2 * t + 2)
                if t >= 2:
                    dve.wait_ge(pe_h2T, 2 * (t - 2) + 2)
                    dve.wait_ge(d_h2[t % 2], 16)
                dve.scalar_tensor_tensor(h2[:, t % 2], x_sb[:, t], rs[:, t:t + 1], g_moe_b, ALU.mult, ALU.mult).then_inc(v_h2, 1)

            def h2T_tile(t):
                dve.wait_ge(pe_h2T, 2 * t + 2)
                dve.tensor_copy(h2T[:, 4:8, tsl(t)], bank[1 + 2 * (t % 2)][:].rearrange("p (c q) -> p c q", q=P)).then_inc(v_h2T, 1)
            h2_tile(0); h2_tile(1); h2T_tile(0); h2_tile(2); h2T_tile(1); h2_tile(3); h2T_tile(2); h2T_tile(3)

            scores, sel, masked, left, chosen, wn, seen, eq = rt
            bias_v = grp[:, 3, 0:E]
            dve.wait_ge(a_sc, 1)
            link(dve.tensor_tensor(sel, scores, bias_v.unsqueeze(1).broadcast_to([P, NT, E]), ALU.add))
            top = grp[:, 0].rearrange("p (a g k) -> p a g k", g=GROUPS, k=8)
            for a_ in range(NT):
                for g in range(GROUPS):
                    ins = dve.max(top[:, a_, g], sel[:, a_, g * PER_GROUP:(g + 1) * PER_GROUP])
            link(ins)
            gs = grp[:, 3, E:E + NT * GROUPS].rearrange("p (a g) -> p a g", g=GROUPS)
            link(dve.tensor_tensor(gs, top[:, :, :, 0], top[:, :, :, 1], ALU.add))
            pair, pair2 = (grp[:, i].rearrange("p (a g k) -> p a g k", g=GROUPS, k=GROUPS) for i in (1, 2))
            for a_ in range(NT):
                me = gs[:, a_].unsqueeze(2).broadcast_to([P, GROUPS, GROUPS])
                other = gs[:, a_].unsqueeze(1).broadcast_to([P, GROUPS, GROUPS])
                dve.tensor_tensor(pair[:, a_], other, me, ALU.is_gt)
                ins = dve.tensor_tensor(pair2[:, a_], other, me, ALU.is_equal)
            link(ins)
            for g in range(GROUPS - 1):
                for_me = pair2[:, :, g, g:GROUPS] if g else pair2[:, :, 0, 0:GROUPS]
                ins = dve.memset(for_me, 0.0)
            link(dve.memset(pair2[:, :, GROUPS - 1, GROUPS - 1:GROUPS], 0.0))
            link(dve.tensor_tensor(pair, pair, pair2, ALU.add))
            place = grp[:, 3, E + 32:E + 64].rearrange("p (a g) -> p a g", g=GROUPS)
            link(dve.tensor_reduce(place, pair, AX.X, ALU.add))
            link(dve.tensor_scalar(gs, place, float(TOPG), None, ALU.is_lt))
            link(dve.tensor_scalar(place, gs, -NEG, NEG, ALU.mult, ALU.add))
            for a_ in range(NT):
                me = sel[:, a_].rearrange("p (g k) -> p g k", k=PER_GROUP)
                mk = masked[:, a_].rearrange("p (g k) -> p g k", k=PER_GROUP)
                link(dve.tensor_tensor(mk, me, gs[:, a_].unsqueeze(2).broadcast_to([P, GROUPS, PER_GROUP]), ALU.mult))
                link(dve.tensor_tensor(mk, mk, place[:, a_].unsqueeze(2).broadcast_to([P, GROUPS, PER_GROUP]), ALU.add))
            for a_ in range(NT):
                link(dve.max(top[:, 0, a_], masked[:, a_]))
                link(dve.match_replace(left[:, a_], top[:, 0, a_], masked[:, a_], 4 * NEG))
            link(dve.tensor_scalar(chosen, left, 2 * NEG, None, ALU.is_lt))
            link(dve.tensor_copy(mask_b[:], chosen))
            dve.tensor_tensor(wn, scores, chosen, ALU.mult).then_inc(v_mask, 1)
            dve.wait_ge(v_mask, 1)
            tot = grp[:, 3, E:E + NT]
            link(dve.tensor_reduce(tot, wn, AX.X, ALU.add))
            link(dve.reciprocal(tot, tot))
            for a_ in range(NT):
                ins = dve.tensor_scalar(wn[:, a_], wn[:, a_], tot[:, a_:a_ + 1], ROUTED_SCALE, ALU.mult, ALU.mult)
            link(ins)
            link(dve.memset(eq, 1.0))
            for a_ in range(NT):
                ins = dve.tensor_tensor_scan(seen[:, a_], eq[:, a_], chosen[:, a_], 0.0, ALU.mult, ALU.add)
            link(ins)
            for j in range(TOPK):
                link(dve.scalar_tensor_tensor(eq, seen, float(j + 1), wn, ALU.is_equal, ALU.mult))
                link(dve.tensor_reduce(wj[:, :, j:j + 1].rearrange("p a c -> p (a c)"), eq, AX.X, ALU.add))
            for c in range(2):
                dve.wait_ge(pe_sh, 3 + c)
                dve.wait_ge(a_ssh, c + 1)
                dve.tensor_tensor(shT[:, c], bank[(7, 0)[c]][:], shT[:, c], ALU.mult).then_inc(v_sh, 1)
            for t in range(NT):
                dve.wait_ge(pe_sd, t + 1)
                b0, b1 = ((1, 2), (3, 5))[t % 2]
                for hf, b in enumerate((b0, b1)):
                    sl = slice(hf * BANK, (hf + 1) * BANK)
                    dve.tensor_tensor(x_sb[:, t, sl], bank[b][:], x_sb[:, t, sl], ALU.add).then_inc(v_base, 1)
            dve.wait_ge(pe_rank, 1)
            dve.wait_ge(p_iota, 1)
            link(dve.scalar_tensor_tensor(rank, bank[6][:, 0:NT * E].rearrange("p (a e) -> p a e", e=E), 1.0, chosen, ALU.add, ALU.mult))
            dve.tensor_scalar(rank, rank, -1.0, None, ALU.add).then_inc(v_rank, 1)
            dve.tensor_scalar(info.rearrange("p e a c -> p c a e")[:, 6], seen, -1.0, None, ALU.add).then_inc(v_rank, 1)

            extra, start, col_e = more[:, 0:1], more[:, 1:2], more[:, 2:3]
            dve.wait_ge(pe_cnt, 1)
            link(dve.tensor_scalar(extra, bank[7][0:E, 0:1], float(SLOTS), None, ALU.is_gt))
            for k in range(2, TILES_MAX):
                link(dve.tensor_scalar(more[:, 3:4], bank[7][0:E, 0:1], float(SLOTS * k), None, ALU.is_gt))
                link(dve.tensor_tensor(extra, extra, more[:, 3:4], ALU.add))
            dve.tensor_copy(more_b[:, 0:1], extra).then_inc(v_more, 1)
            dve.wait_ge(pe_st, 1)
            link(dve.tensor_copy(start, bank[7][0:E, 8:9]))
            dve.wait_ge(p_iota, 1)
            hot = [rt[i][0:E, 0] for i in range(1, 6)]
            val = rt[6][0:E, 0]
            for k in range(1, TILES_MAX):
                link(dve.tensor_scalar(more[:, 4:5], start, float(k - 1), None, ALU.add))
                link(dve.tensor_scalar(more[:, 5:6], extra, float(k), None, ALU.is_ge))
                link(dve.tensor_scalar(hot[k - 1], iota[0:E, 0:E], more[:, 4:5], more[:, 5:6], ALU.is_equal, ALU.mult))
            for k in range(1, TILES_MAX):
                link(dve.memset(val[:, k:k + 1], float(k * SLOTS)))
            dve.tensor_copy(val[:, 0:1], tcol[0:E, 0:1]).then_inc(v_hot, 1)
            dve.wait_ge(pe_tab, 1)
            dve.tensor_copy(table[0:1, 0], bank[7][0:1, E:2 * E]).then_inc(v_tab, 1)
            dve.tensor_copy(table[0:1, 1], bank[7][0:1, 2 * E:3 * E]).then_inc(v_tab, 1)
            dve.tensor_copy(table[0:1, 2, 0:1], bank[7][0:1, 16:17]).then_inc(v_tab, 1)

            def one_hot(i, e=None, k=0):
                e = i.n if e is None else e
                if not (isinstance(i.n, int) and i.n < 2):
                    dve.wait_ge(pe_info, i.n - i.lag2 + 1)
                dve.tensor_copy(info_t[:, i.s2], info[:, bass.ds(e, 1)].rearrange("p e a c -> p (e a c)"))
                dve.tensor_tensor(
                    onehot[:, i.s2], iota[:, bass.ds(k, SLOTS)].unsqueeze(1).broadcast_to([P, NT, SLOTS]),
                    rank[:, :, bass.ds(e, 1)].broadcast_to([P, NT, SLOTS]), ALU.is_equal).then_inc(v_oh, 1)

            def index(i):
                dve.wait_ge(pe_info, i.n + 1)
                if not (isinstance(i.n, int) and i.n < RING):
                    dve.wait_ge(d_sc[i.s2], 16 * (i.uses2 - i.sc_before))
                dve.tensor_reduce(idx_f[:, i.s2], bank[7][0:SLOTS, 0:8].rearrange("p (w c) -> p w c", c=4), AX.X, ALU.add).then_inc(v_idf, 1)
                dve.wait_ge(v_idf, i.n + 1)
                dve.tensor_scalar(idx[:, i.s4], idx_f[:, i.s2], NO_ROW, None, ALU.add).then_inc(v_idx, 1)

            def xT_tile(i):
                dve.wait_ge(pe_T, i.n + 1)
                if not (isinstance(i.n, int) and i.n < 2):
                    dve.wait_ge(pe_gu, i.n - i.lag2 + 1)
                dve.tensor_copy(xT[:, i.s2, 4:8], bank[1][:, 0:4 * SLOTS].rearrange("p (k s) -> p k s", s=SLOTS)).then_inc(v_xT, 1)

            def hidden(i):
                dve.wait_ge(a_sg, i.n + 1)
                if not (isinstance(i.n, int) and i.n < 2):
                    dve.wait_ge(pe_dn, i.n - i.lag2 + 1)
                dve.tensor_tensor(hidT[:, i.s2], bank[2 + i.s2][:, 2 * SLOTS:4 * SLOTS].rearrange("p (c s) -> p c s", s=SLOTS),
                                  sg[:, i.s2], ALU.mult).then_inc(v_hid, 1)

            def y_tile(i):
                dve.wait_ge(pe_dn, i.n + 1)
                if not (isinstance(i.n, int) and i.n < 2):
                    dve.wait_ge(d_sc[i.s2], 16 * (i.uses2 - 1))
                dve.tensor_copy(y_sb[0:SLOTS, i.s2, BANK:D], bank[5][0:SLOTS, :]).then_inc(v_y, 1)

            def mid(i):
                n2, n3 = shift(i, 2), shift(i, 3)
                if n2 is not None:
                    index(n2)
                hidden(i)
                if n3 is not None:
                    one_hot(n3)
            dve.wait_ge(v_rank, 2)
            one_hot(item(0, 0))
            one_hot(item(0, 1))
            one_hot(item(0, 2))
            index(item(0, 0))
            index(item(0, 1))
            pipeline(dve, xT_tile, mid, y_tile)

            def over(i, j):
                e = dve.value_load(table[0:1, 0, bass.ds(j, 1)], min_val=0, max_val=E - 1)
                k = dve.value_load(table[0:1, 1, bass.ds(j, 1)], min_val=0, max_val=(TILES_MAX - 1) * SLOTS)
                one_hot(i, e, k)
                index(i)
                xT_tile(i)
                hidden(i)
                y_tile(i)
            overflow_loop(dve, over)

            for t in range(NT):
                dve.wait_ge(d_y[t % 2], 16 * (t // 2 + 1))
                for j in range(TOPK):
                    ins = dve.scalar_tensor_tensor(x_sb[:, t], y_in[t % 2][:, j], wj[:, t, j:j + 1], x_sb[:, t], ALU.mult, ALU.add)
                    if j < TOPK - 1:
                        link(ins)
                ins.then_inc(v_comb, 1)
                dve.wait_ge(p_rs3, t + 1)
                dve.wait_ge(d_ple, 48)
                if t >= 2:
                    dve.wait_ge(pe_h3T, t - 1)
                dve.scalar_tensor_tensor(h3[:, t % 2], x_sb[:, t], rs[:, t:t + 1], g_ple_b, ALU.mult, ALU.mult).then_inc(v_h3, 1)
                dve.wait_ge(pe_h3T, t + 1)
                if t >= 2:
                    dve.wait_ge(pe_pg, t - 1)
                dve.tensor_copy(h3T[:, t % 2, 4:8], bank[1 + 2 * (t % 2)][:].rearrange("p (c q) -> p c q", q=P)).then_inc(v_h3T, 1)
                if t >= 1:
                    tail_bias(dve, t - 1)
            tail_bias(dve, NT - 1)

        @block.tensor
        def _(pe):
            mm, tp = pe.matmul, pe.transpose

            pe.wait_ge(p_pos, 1)
            pe.wait_ge(d_small, 16 * N_SMALL)
            tp(bank[7][:, 0:2 * KD], rows[:], ident[0:2 * KD, 0:2 * KD])
            tp(bank[7][:, 2 * KD:2 * KD + NT], pos_f[:], ident[0:NT, 0:NT]).then_inc(pe_rows, 1)
            pe.wait_ge(d_p, 32)
            pe.wait_ge(v_cols, 1)
            for t in range(NT):
                for c in range(2):
                    ins = tp(bank[4 + t][:, c * P:(c + 1) * P], p_sb[:, t, c * P:(c + 1) * P], ident[:])
                ins.then_inc(pe_pT, 1)
            for t in range(NT):
                pe.wait_ge(a_pT, t + 1)
                if t >= 2:
                    pe.wait_ge(a_pp, t - 1)
                    pe.wait_ge(v_pp, t - 1)
                for hf in range(2):
                    for c in range(2):
                        ins = mm(bank[2 * (t % 2) + hf][:], pT[:, c, tsl(t)], w_pp[:, c, hf * BANK:(hf + 1) * BANK],
                                 start=c == 0, stop=c == 1)
                ins.then_inc(pe_pp, 1)
            pe.wait_ge(a_pT, NT)
            for t in range(NT):
                pe.wait_ge(v_xn, t + 1)
                if t >= 2:
                    pe.wait_ge(a_hT, t - 1)
                    pe.wait_ge(v_hT, t - 1)
                for k in range(KD):
                    ins = tp(bank[4 + 2 * (t % 2) + k // 4][:, (k % 4) * P:(k % 4 + 1) * P], xn[:, t % 2, tsl(k)], ident[:])
                    if k % 4 == 3:
                        ins.then_inc(pe_hT, 1)

            def z_tile(t):
                for k in range(KD):
                    pe.wait_ge(d_w1[k], 16)
                    for c in range(3):
                        ins = mm(bank[3 * (t % 2) + c][:, 0:Z_CHUNK], hT[:, k, tsl(t)], w1[:, k, c * Z_CHUNK:(c + 1) * Z_CHUNK],
                                 start=k == 0, stop=k == KD - 1)
                ins.then_inc(pe_z, 1)

            def cT_tile(t):
                pe.wait_ge(v_cn, t + 1)
                if t:
                    pe.wait_ge(a_cT, t)
                    pe.wait_ge(v_cT, t)
                for c in range(C_BLOCKS):
                    dst = bank[6][:, c * P:(c + 1) * P] if c < 4 else bank[7][:, 0:P]
                    ins = tp(dst, c_n[:, t % 2, c * P:(c + 1) * P], ident[:])
                ins.then_inc(pe_cT, 1)

            def up_tile(t):
                if t:
                    pe.wait_ge(a_up, 2 * t)
                    pe.wait_ge(v_up, 2 * t)
                n = MH * QK // 2
                for hf in range(2):
                    for c in range(Q_BLOCKS):
                        mm(bank[hf][:, 0:n], cT[:, c, tsl(t)], wuq[:, c, hf * n:(hf + 1) * n], start=c == 0, stop=c == Q_BLOCKS - 1)
                for hf in range(2):
                    for c in range(2):
                        ins = mm(bank[2 + hf][:], cT[:, Q_BLOCKS + c, tsl(t)], wukv[:, c, hf * BANK:(hf + 1) * BANK],
                                 start=c == 0, stop=c == 1)
                ins.then_inc(pe_up, 1)

            def gate(c):
                g = c // 2
                pe.wait_ge(d_wg[g % 3], 16 * (g // 3 + 1))
                if c >= 2:
                    pe.wait_ge(a_g, c - 1)
                for k in range(KD):
                    ins = mm(bank[4 + c % 2][:], w_g[g % 3][:, k, (c % 2) * P:(c % 2 + 1) * P], hT[:, k, :], start=k == 0, stop=k == KD - 1)
                ins.then_inc(pe_g, 1)

            for s_, n_ in ((a_hT, NT), (v_hT, NT), (a_pp, NT), (v_pp, NT)):
                pe.wait_ge(s_, n_)
            z_tile(0); z_tile(1); cT_tile(0)
            pe.wait_ge(a_z, 2); pe.wait_ge(v_z, 1)
            z_tile(2); cT_tile(1)
            pe.wait_ge(a_z, 4); pe.wait_ge(v_z, 2)
            z_tile(3); cT_tile(2)
            pe.wait_ge(a_z, 2 * NT); pe.wait_ge(v_z, NT)
            gate(0); cT_tile(3)
            pe.wait_ge(a_cT, NT); pe.wait_ge(v_cT, NT); pe.wait_ge(d_wu, 32)
            for t in range(NT):
                up_tile(t)
                if t < 3:
                    gate(t + 1)
            for c in range(4, 2 * KD):
                gate(c)

            pe.wait_ge(v_nrm, NT)
            pe.wait_ge(p_prep, NT)
            for j in range(22):
                if j == 0:
                    pe.wait_ge(a_up, 2 * NT); pe.wait_ge(v_up, 2 * NT)
                if j >= 4:
                    pe.wait_ge((a_tr, v_tr)[j % 2], (j - 4) // 2 + 1)
                for t in range(NT):
                    if j < 8:
                        src = q_sb[:, t, j * QK:(j + 1) * QK]
                    elif j < 16:
                        src = kk[:, t, (j - 8) * QK:(j - 7) * QK]
                    elif j < 20:
                        src = z[:, t, C_QS + (j - 16) * P:C_QS + (j - 15) * P]
                    else:
                        src = k_dup[:, t, (j - 20) * P:(j - 19) * P]
                    ins = tp(bank[j % 4][0:src.shape[1], tsl(t)], src, ident[:])
                ins.then_inc(pe_tr, 1)

            pe.wait_ge(a_tr, 11); pe.wait_ge(v_tr, 11); pe.wait_ge(a_g, 2 * KD)

            def scores(u):
                qt, kind, h = units[u]
                if u >= 3:
                    pe.wait_ge(a_e, u - 2)
                b = bank[u % 3]
                if kind == 0:
                    ins = mm(b[:], qT[0:QK, h, tsl(qt)], kT[0:QK, h], start=True, stop=True)
                else:
                    lo, n = band(qt)
                    r = slice(HD * (h % 2), HD * (h % 2) + HD)
                    masks = ([(0, 0)] if qt > 0 else []) + ([(n - 1, 1)] if qt < NT - 1 else [])
                    mm(b[:, 0:n * P], qwT[r, h // 2, tsl(qt)], kwT[r, h // (WH // WKV), lo * P:(lo + n) * P],
                       start=True, stop=False)
                    for x_, (blk, m) in enumerate(masks):
                        ins = mm(b[:, blk * P:(blk + 1) * P], ident_b[:], band_b[:, m], start=False, stop=x_ == len(masks) - 1)
                ins.then_inc(pe_s, 1)

            def transposes(u):
                qt, kind, h = units[u]
                pe.wait_ge(a_e, u + 1)
                if u >= 2:
                    pe.wait_ge((a_pt, v_pt)[u % 2], (u - 2) // 2 + 1)
                for b in range(NT if kind == 0 else band(qt)[1]):
                    ins = tp(bank[3 + u % 2][:, tsl(b)], prob[:, u % 2, tsl(b)], ident[:])
                ins.then_inc(pe_t, 1)

            def values(u):
                qt, kind, h = units[u]
                g = u // 8
                pe.wait_ge((a_pt, v_pt)[u % 2], u // 2 + 1)
                if h == 0 and g >= 2:
                    pe.wait_ge(v_o, g - 1)
                lo, n = (0, NT) if kind == 0 else band(qt)
                for b in range(n):
                    v = (kv[:, lo + b, h * (NOPE + VD) + NOPE:(h + 1) * (NOPE + VD)] if kind == 0 else
                         z[:, lo + b, C_VS + HD * (h // (WH // WKV)):C_VS + HD * (h // (WH // WKV) + 1)])
                    ins = mm(bank[5 + g % 2][:, h * VD:(h + 1) * VD], probT[:, u % 2, tsl(b)], v, start=b == 0, stop=b == n - 1)
                ins.then_inc(pe_pv, 1)

            def out_transposes(g):
                pe.wait_ge(v_o, g + 1)
                if g:
                    pe.wait_ge(a_oT, g)
                for c in range(4):
                    ins = tp(bank[7][:, tsl(c)], o_sb[:, tsl(c)], ident[:])
                ins.then_inc(pe_ot, 1)

            for i in range(UNITS + 16):
                if i < UNITS:
                    scores(i)
                if 0 <= i - 2 < UNITS:
                    transposes(i - 2)
                if 0 <= i - 3 < UNITS:
                    values(i - 3)
                if i >= 12 and (i - 12) % 8 == 0 and (i - 12) // 8 < 2 * NT:
                    out_transposes((i - 12) // 8)

            pe.wait_ge(a_oT, 2 * NT)
            pe.wait_ge(d_bm, 16); pe.wait_ge(d_bs, 16)
            for c in range(KD):
                if c >= 2:
                    pe.wait_ge(v_br, c - 1)
                for w, o, b in ((w_bm, oT_m, bank[c % 2]), (w_bs, oT_w, bank[2 + c % 2])):
                    for k in range(4):
                        ins = mm(b[:], w[:, k, tsl(c)], o[:, k], start=k == 0, stop=k == 3)
                ins.then_inc(pe_br, 1)
            pe.wait_ge(v_mT, KD); pe.wait_ge(d_wo, 16)
            for t in range(NT):
                if t >= 2:
                    pe.wait_ge(v_x1, 2 * (t - 1))
                for k in range(KD):
                    for hf in range(2):
                        ins = mm(bank[4 + 2 * (t % 2) + hf][:], mT[:, k, tsl(t)], w_o[:, k, hf * BANK:(hf + 1) * BANK],
                                 start=k == 0, stop=k == KD - 1)
                ins.then_inc(pe_wo, 1)
            for t in range(NT):
                pe.wait_ge(v_h2, t + 1)
                if t >= 2:
                    pe.wait_ge(a_h2T, t - 1)
                    pe.wait_ge(v_h2T, t - 1)
                for k in range(KD):
                    ins = tp(bank[2 * (t % 2) + k // 4][:, (k % 4) * P:(k % 4 + 1) * P], h2[:, t % 2, tsl(k)], ident[:])
                    if k % 4 == 3:
                        ins.then_inc(pe_h2T, 1)
            pe.wait_ge(d_wr, 48); pe.wait_ge(v_x1, 2 * NT)
            pe.wait_ge(a_h2T, NT); pe.wait_ge(v_h2T, NT)
            for t in range(NT):
                for k in range(KD):
                    ins = mm(bank[4][:, t * E:(t + 1) * E], h2T[:, k, tsl(t)], w_r[:, k], start=k == 0, stop=k == KD - 1)
            ins.then_inc(pe_lg, 1)
            pe.wait_ge(d_sg, 16)
            for c in range(4):
                for k in range(KD):
                    ins = mm(bank[(5, 6, 7, 0)[c]][:], w_sg[:, k, tsl(c)], h2T[:, k], start=k == 0, stop=k == KD - 1)
                ins.then_inc(pe_sh, 1)
            pe.wait_ge(v_mask, 1)
            pe.wait_ge(a_ssh, 2); pe.wait_ge(v_sh, 2)
            pe.wait_ge(d_sd, 16)
            for t in range(NT):
                for s in range(t + 1):
                    ins = mm(bank[6][:, t * E:(t + 1) * E], (before_b if s == t else ones_b)[:], mask_b[:, s], start=s == 0, stop=s == t)
            ins.then_inc(pe_rank, 1)
            for t in range(NT):
                ins = mm(bank[7][0:E, 0:1], mask_b[:, t], ones_b[:, 0:1], start=t == 0, stop=t == NT - 1)
            ins.then_inc(pe_cnt, 1)
            for t in range(NT):
                if t >= 2:
                    pe.wait_ge(v_base, 2 * (t - 1))
                for hf in range(2):
                    for c in range(2):
                        ins = mm(bank[((1, 2), (3, 5))[t % 2][hf]][:], shT[:, c, tsl(t)], w_sd[:, c, hf * BANK:(hf + 1) * BANK],
                                 start=c == 0, stop=c == 1)
                ins.then_inc(pe_sd, 1)
            pe.wait_ge(v_more, 1)
            mm(bank[7][0:E, 8:9], before_b[0:E, 0:E], more_b[:, 0:1], start=True, stop=True)
            mm(bank[7][0:1, 16:17], more_b[:, 0:1], ones_b[0:E, 0:1], start=True, stop=True).then_inc(pe_st, 1)
            pe.wait_ge(v_hot, 1)
            hot = [rt[i][0:E, 0] for i in range(1, 6)]
            val = rt[6][0:E, 0]
            for w in range(2):
                for k in range(1, TILES_MAX):
                    c = 0 if w == 0 else k
                    ins = mm(bank[7][0:1, E * (1 + w):E * (2 + w)], val[:, c:c + 1], hot[k - 1], start=k == 1, stop=k == TILES_MAX - 1)
            ins.then_inc(pe_tab, 1)
            pe.wait_ge(v_tab, 3)
            pe.wait_ge(v_base, 2 * NT)

            def early(i, n):
                return isinstance(i.n, int) and i.n < n

            def info_of(i):
                pe.wait_ge(v_oh, i.n + 1)
                if not early(i, 1):
                    pe.wait_ge(v_idx, i.n)
                for a_ in range(NT):
                    ins = mm(bank[7][0:SLOTS, 0:8], onehot[:, i.s2, a_], info_t[:, i.s2, a_ * 8:(a_ + 1) * 8], start=a_ == 0, stop=a_ == NT - 1)
                ins.then_inc(pe_info, 1)

            def turn(i):
                pe.wait_ge(d_xg[i.s2], 16 * i.uses2)
                if not early(i, 1):
                    pe.wait_ge(a_xT, i.n)
                    pe.wait_ge(v_xT, i.n)
                for k in range(KD):
                    ins = tp(bank[k // 4][:, (k % 4) * SLOTS:(k % 4 + 1) * SLOTS], xg[0:SLOTS, i.s2, tsl(k)], ident[0:SLOTS, 0:SLOTS])
                ins.then_inc(pe_T, 1)

            def gate_up(i):
                pe.wait_ge(a_xT, i.n + 1)
                pe.wait_ge(v_xT, i.n + 1)
                pe.wait_ge(d_gu[i.s4], 16 * i.uses4)
                if not early(i, 2):
                    pe.wait_ge(v_hid, i.n - i.lag2 + 1)
                for c in range(4):
                    for k in range(KD):
                        ins = mm(bank[2 + i.s2][:, c * SLOTS:(c + 1) * SLOTS], w_gu[i.s4][:, k, tsl(c)], xT[:, i.s2, k], start=k == 0, stop=k == KD - 1)
                ins.then_inc(pe_gu, 1)

            def down(i):
                pe.wait_ge(v_hid, i.n + 1)
                pe.wait_ge(d_dn[i.s4], 16 * i.uses4)
                if not early(i, 1):
                    pe.wait_ge(a_y, i.n)
                    pe.wait_ge(v_y, i.n)
                for c in range(2):
                    for hf in range(2):
                        ins = mm(bank[4 + hf][0:SLOTS, :], hidT[:, i.s2, c], w_dn[i.s4][:, c, hf * BANK:(hf + 1) * BANK], start=c == 0, stop=c == 1)
                ins.then_inc(pe_dn, 1)

            def step(it, s):
                i, known = item(it, s), isinstance(it, int)
                n2 = shift(i, 2)
                if n2 is not None:
                    info_of(n2)
                gate_up(i)
                n1 = shift(i, 1)
                if n1 is not None:
                    turn(n1)
                if not known or i.n >= 1:
                    down(item(it + (s - 1) // RING, (s - 1) % RING))
            info_of(item(0, 0))
            info_of(item(0, 1))
            turn(item(0, 0))
            for s in range(RING):
                step(0, s)
            with pe.Fori(1, E // RING - 1) as it:
                for s in range(RING):
                    step(it, s)
            for s in range(RING):
                step(E // RING - 1, s)
            down(item(E // RING - 1, RING - 1))

            def over(i, j):
                info_of(i)
                turn(i)
                gate_up(i)
                down(i)
            overflow_loop(pe, over)

            pe.wait_ge(d_ple, 48)
            for t in range(NT):
                pe.wait_ge(v_h3, t + 1)
                if t >= 2:
                    pe.wait_ge(a_h3T, t - 1)
                    pe.wait_ge(v_h3T, t - 1)
                for k in range(KD):
                    ins = tp(bank[2 * (t % 2) + k // 4][:, (k % 4) * P:(k % 4 + 1) * P], h3[:, t % 2, tsl(k)], ident[:])
                ins.then_inc(pe_h3T, 1)
                pe.wait_ge(a_h3T, t + 1)
                pe.wait_ge(v_h3T, t + 1)
                if t >= 2:
                    pe.wait_ge(v_gb, t - 1)
                for k in range(KD):
                    for hf in range(2):
                        ins = mm(bank[4 + 2 * (t % 2) + hf][:], h3T[:, t % 2, k], w_pg[:, k, hf * BANK:(hf + 1) * BANK],
                                 start=k == 0, stop=k == KD - 1)
                ins.then_inc(pe_pg, 1)


_INS = ["x", "p", "positions", "g_mix", "w_in", "b_gate", "g_cq", "w_uq", "g_ckv", "w_ukv", "g_qn_mla", "g_kn_mla",
        "g_qn_swa", "g_kn_swa", "sink", "w_br_mla", "w_br_swa", "w_out", "g_moe", "w_router", "router_bias",
        "w_exp_gu", "w_exp_down", "w_sh_gu", "w_sh_down", "g_ple", "w_ple_gate", "b_ple", "w_ple_proj"]


def kernel(**inputs):
    import numpy as _np
    import concourse.bacc as _bacc
    from concourse import mybir as _mybir
    from concourse.bass_utils import run_bass_kernel_spmd as _run

    nc = _bacc.Bacc("TRN2", target_bir_lowering=False, num_devices=1)
    arrays, args = {}, []
    for name in _INS:
        arrays[f"in_{name}"] = _np.ascontiguousarray(inputs[name])
    arrays["in_rope_freq"] = _np.concatenate([
        _np.float32(1.0) / _np.float32(THETA) ** (_np.arange(0, n, 2, dtype=_np.float32) / _np.float32(n))
        for n in (ROPE, HD)]).astype(_np.float32).reshape(1, NF)
    for name, a in arrays.items():
        args.append(nc.dram_tensor(name, a.shape, _mybir.dt.from_np(a.dtype), kind="ExternalInput").ap())
    args.append(nc.dram_tensor("out_0", (1, T, D), _mybir.dt.float32, kind="ExternalOutput").ap())
    build(nc, *args)
    r = _run(nc, [arrays], core_ids=[0])
    return r.results[0]["out_0"]
```

```python
import math
from contextlib import ExitStack

import concourse.bass as bass
from concourse import mybir

P = 128
BANK = 512
T, D = 512, 1024
NT, KD = T // P, D // P
PLE = 256
EPS = 1e-6
THETA = 10000.0
NEG = -1e30

MH, Q_RANK, KV_RANK, NOPE, ROPE, VD = 8, 384, 256, 64, 32, 64
QK = NOPE + ROPE
WH, WKV, HD = 8, 2, 64
C_CKV = Q_RANK
C_KR = C_CKV + KV_RANK
C_QS = C_KR + ROPE
C_KS = C_QS + WH * HD
C_VS = C_KS + WKV * HD
C_GATE = C_VS + WKV * HD
IN_W = C_GATE + 2 * D
Z_CHUNK = C_GATE // 3
C_BLOCKS = (Q_RANK + KV_RANK) // P
Q_BLOCKS = Q_RANK // P

E, TOPK, GROUPS, TOPG = 64, 8, 8, 4
PER_GROUP = E // GROUPS
FF, SH = 256, 256
ROUTED_SCALE = 2.5
SLOTS = 96
TILES_MAX = -(-T // SLOTS)
RING = 4
GROUP = 8
ARENA = 50816
NO_ROW = 32768.0
UNITS = 2 * NT * 8

ROUND = 12582912.0
TWO_PI = (201.0 / 32, 8117.0 / 2 ** 22, 2 * math.pi - 201.0 / 32 - 8117.0 / 2 ** 22)

F_M, F_S = ROPE // 2, HD // 2
NF = F_M + F_S


def build(nc, x, p, positions, g_mix, w_in, b_gate, g_cq, w_uq, g_ckv, w_ukv, g_qn_mla, g_kn_mla,
          g_qn_swa, g_kn_swa, sink, w_br_mla, w_br_swa, w_out, g_moe, w_router, router_bias,
          w_exp_gu, w_exp_down, w_sh_gu, w_sh_down, g_ple, w_ple_gate, b_ple, w_ple_proj,
          rope_freq, out):
    f32, f32r, bf16, i32, u32 = mybir.dt.float32, mybir.dt.float32r, mybir.dt.bfloat16, mybir.dt.int32, mybir.dt.uint32
    ALU, ACT, AX = mybir.AluOpType, mybir.ActivationFunctionType, mybir.AxisListType

    with ExitStack() as ctx:
        def sb(name, shape, dt=f32):
            return ctx.enter_context(nc.sbuf_tensor(name, shape, dt))

        def sem(name):
            return ctx.enter_context(nc.semaphore(name))

        h_rows = nc.dram_tensor("h_rows", [T, D], f32).ap()
        y_rows = nc.dram_tensor("y_rows", [T * TOPK, D], f32).ap()
        pp_rows = nc.dram_tensor("pp_rows", [T, D], f32).ap()

        def cut(memory, at, *dims):
            n = math.prod(dims)
            v = memory[:, at:at + n]
            if len(dims) == 2:
                v = v.rearrange("p (a b) -> p a b", b=dims[1])
            if len(dims) == 3:
                v = v.rearrange("p (a b c) -> p a b c", b=dims[1], c=dims[2])
            return v

        def split(name, at, *dims):
            with nc.sbuf_tensor(name + "_below", [P, at], f32), nc.sbuf_tensor(name, [P, math.prod(dims)], f32r) as memory:
                return cut(memory, 0, *dims)


        w_hi = [split(f"w_hi{s}", 28672 + 2048 * s, FF // P, D) for s in range(2)]
        w_lo = [split(f"w_lo{s}", 20480 + 2048 * s, FF // P, D) for s in range(RING)]
        hid_hi = split("hid_hi", 32768, 2, FF // P, SLOTS)
        hid_lo = split("hid_lo", 33152, 2, FF // P, SLOTS)
        wo_hi = [split(f"wo_hi{i}", at, 2, D) for i, at in enumerate((39808, 41856, 26240, 28288))]
        wo_lo = [split(f"wo_lo{i}", 8192 + 2048 * i, 2, D) for i in range(KD // 2)]
        pg_hi = [split(f"pg_hi{i}", at, 2, D) for i, at in enumerate((16384, 18432, 22528, 24576))]
        pg_lo = [split(f"pg_lo{i}", 8192 + 2048 * i, 2, D) for i in range(KD // 2)]
        h3_hi = [split(f"h3_hi{b}", 34816 + 1024 * b, KD, P) for b in range(2)]
        h3_lo = split("h3_lo", 49024, KD, P)
        h_hi = [split(f"h_hi{i}", 39808 + 2048 * i, 4, T) for i in range(2)]
        h_lo = [split(name, at, n, T) for name, at, n in (("h_lo0", 43904, 3), ("h_lo1", 45440, 2), ("h_lo2", 6656, 3))]
        wg_hi = [split(f"wg_hi{b}", 18048 + 1024 * b, KD, P) for b in range(2)]
        wg_lo = [split(f"wg_lo{b}", 13952 + 2048 * b, KD, 2 * P) for b in range(2)]
        m_hi = [split(f"m_hi{c}", 16384 + BANK * c if c < KD - 1 else 30336, T) for c in range(KD)]
        m_lo = [split(f"m_lo{c}", 4096 + BANK * c, T) for c in range(KD)]
        arena = sb("arena", [P, ARENA])

        def view(at, *dims):
            return cut(arena, at, *dims)


        x_sb = view(0, NT, D)
        hT = view(4096, KD, T)
        z = view(8192, NT, C_GATE)
        w_g = [view(13952 + 2048 * s, KD, 2 * P) for s in range(2)]
        w1 = view(20096, KD, C_GATE)
        q_sb = view(20096, NT, MH * QK)
        kk = view(23168, NT, MH * QK)
        kv = view(26240, NT, MH * (NOPE + VD))
        gT = view(31616, 2 * KD, T)
        cT = view(39808, C_BLOCKS, T)
        wuq = view(42368, Q_BLOCKS, MH * QK)
        wukv = view(44672, KV_RANK // P, MH * (NOPE + VD))
        xn = view(46720, 2, D)
        g_mix_b = view(48768, D)
        sq = view(46720, 1952)
        rope_t = view(48672, 4, 320)
        g_cq_b = view(49952, Q_RANK)
        g_ckv_b = view(50336, KV_RANK)
        c_n = view(48672, 2, C_BLOCKS * P)
        ang = view(39808, 6, NT * NF)
        ssq = view(31360, 2, 32)
        rsq = view(31424, 2, 32)
        p_sb = view(31616, NT, PLE)
        pT = view(32640, PLE // P, T)
        w_pp = view(33664, PLE // P, D)
        pp_st = view(35712, NT, D)
        qT = view(4096, MH, T)
        kT = view(13952, MH, T)
        prob = view(18048, 2, T)
        probT = view(19072, 2, NT * P)
        qwT = view(39808, WH // 2, T)
        k_dup = view(30336, NT, 2 * WKV * HD)
        kwT = view(42880, WKV, T)
        oT_w = view(43904, NT, T)
        o_sb = view(45952, MH * VD)
        oT_m = view(24192, NT, T)
        w_bm = view(20096, MH * VD // P, D)
        w_bs = view(46720, WH * HD // P, D)
        mT = view(4096, KD, T)
        w_o = view(8192, KD, D)
        br_t = view(45952, T)
        g_moe_b = view(20096, D)
        h2 = view(21120, 2, D)
        junk2 = view(23168, D)
        h2T = view(31616, KD, T)
        w_sg = view(26240, KD, 2 * SH)
        w_sd = view(35712, SH // P, D)
        w_r = view(37760, KD, E)
        shT = view(38272, SH // P, T)
        rt = [view(46720 + 256 * i, NT, E) for i in range(8)]
        info = arena[:, 48768:49792].bitcast(bf16).rearrange("p (e a c) -> p e a c", a=NT, c=8)
        grp = view(49792, 4, 256)
        tab_t = view(33536, TILES_MAX, E)
        w_gu = [view(4096 * (1 + s), KD, 2 * FF) for s in range(RING)]
        w_dn = [view(20480 + 2048 * s, FF // P, D) for s in range(RING)]
        w_pg = view(8192, KD, D)
        g_ple_b = view(36864, D)
        b_ple_b = view(37888, D)
        iota = view(49792, TILES_MAX * SLOTS)
        iot_i = arena[:, 41856:41856 + TILES_MAX * SLOTS].bitcast(i32)
        rank = view(39488, NT, E)
        xg = [view(at, D) for at in (39808, 40832, 46720, 47744)]
        xT = view(41856, 2, KD, SLOTS)
        hidT = view(43392, 2, FF // P, SLOTS)
        sg = view(43776, 2, FF // P, SLOTS)
        y_sb = view(44160, 2, D)
        onehot = arena[:, 46208:46592].bitcast(bf16).rearrange("p (r a s) -> p r a s", r=2, a=NT)
        y_in = [view(at, 2, D) for at in (20480, 26624, 28672, 30720)]
        h3 = view(32768, 2, D)
        gate3 = view(4096, 2, D)
        out_st = view(6144, 2, D)
        pp_in = view(40832, NT, D)
        junk3 = view(39808, D)

        ident = sb("ident", [P, P])
        ident_b = sb("ident_b", [P, P], bf16)
        before_b = sb("before_b", [P, P], bf16)
        ones_b = sb("ones_b", [P, P], bf16)
        band_b = sb("band_b", [P, 2, P], bf16)
        rows = sb("rows", [2 * KD, P])
        pos_f = sb("pos_f", [NT, P])
        pos_i = sb("pos_i", [NT, P], i32)
        cols = sb("cols", [P, 2 * KD + NT])
        freq = sb("freq", [P, NF])
        cs = sb("cs", [P, 2, NT, NF])
        g_q = sb("g_q", [P, QK])
        g_k = sb("g_k", [P, QK])
        g_s = sb("g_s", [P, 2, HD])
        sink_b = sb("sink_b", [P, WH])
        ssum = sb("ssum", [P, 32])
        rs = sb("rs", [P, 32])
        half = sb("half", [P, 32])
        nmax = sb("nmax", [P, UNITS])
        lsum = sb("lsum", [P, UNITS])
        es = sb("es", [P, 2 * WH])
        wj = sb("wj", [P, NT, TOPK])
        idx = sb("idx", [SLOTS, GROUP, 2], u32)
        idx_f = sb("idx_f", [SLOTS, 2, 2])
        info_t = sb("info_t", [P, 2, NT * 8], bf16)
        more = sb("more", [E, 4 * 8])
        more_b = sb("more_b", [E, 2], bf16)
        table = sb("table", [1, 3, E], i32)
        rtmp = sb("rtmp", [P, 32])
        mx1 = sb("mx1", [P, 2])
        tcol = sb("tcol", [P, 2])
        mask_b = sb("mask_b", [P, NT, E], bf16)
        kr_t = view(50592, 6, F_M)
        bank = [ctx.enter_context(nc.psum_tensor(f"bank{b}", [P, BANK], f32)) for b in range(8)]

        d_small, d_p, d_wu, d_br, d_pg, d_wo, d_sg, d_sd, d_wr, d_ple = [
            sem(n) for n in ("d_small", "d_p", "d_wu", "d_br", "d_pg", "d_wo", "d_sg", "d_sd", "d_wr", "d_ple")]
        d_x = [sem(f"d_x{t}") for t in range(NT)]
        d_w1 = [sem(f"d_w1_{k}") for k in range(KD // 2)]
        d_wg = [sem(f"d_wg{s}") for s in range(2)]
        d_pps = sem("d_pps")
        d_h2 = [sem(f"d_h2_{s}") for s in range(2)]
        d_gu = [sem(f"d_gu{s}") for s in range(RING)]
        d_dn = [sem(f"d_dn{s}") for s in range(RING)]
        d_xg = [sem(f"d_xg{s}") for s in range(RING)]
        d_sc = [sem(f"d_sc{s}") for s in range(2)]
        d_y = [sem(f"d_y{s}") for s in range(4)]
        d_ppi = sem("d_ppi")
        d_out = [sem(f"d_out{s}") for s in range(2)]
        (pe_rows, pe_pT, pe_pp, pe_hT, pe_z, pe_cT, pe_up, pe_g, pe_tr, pe_s, pe_t, pe_pv, pe_ot, pe_br, pe_wo,
         pe_h2T, pe_lg, pe_sh, pe_sd, pe_rank, pe_st, pe_tab, pe_info, pe_T, pe_gu, pe_dn, pe_h3T,
         pe_pg) = [sem("pe_" + n) for n in (
             "rows pT pp hT z cT up g tr s t pv ot br wo h2T lg sh sd rank st tab info T gu dn h3T pg").split()]
        (a_pT, a_ss, a_pp, a_hT, a_z, a_c, a_cT, a_up, a_g, a_sq, a_trig, a_tr, a_e, a_pt, a_es, a_oT, a_h2T,
         a_sc, a_ssh, a_xT, a_sg, a_y, a_h3T, a_gate, a_pg, a_hi, a_half) = [sem("a_" + n) for n in (
             "pT ss pp hT z c cT up g sq trig tr e pt es oT h2T sc ssh xT sg y h3T gate pg hi half").split()]
        (v_cols, v_xn, v_pp, v_hT, v_z, v_cn, v_cT, v_up, v_trig, v_red, v_nrm, v_tr, v_nm, v_pt, v_es, v_o, v_br,
         v_mT, v_x1, v_h2, v_h2T, v_sh, v_base, v_mask, v_rank, v_more, v_hot, v_tab, v_idx, v_xT, v_hid, v_y,
         v_comb, v_h3, v_out, v_gb, v_step, v_idf, v_oh, v_lo, v_hp, v_half) = [sem("v_" + n) for n in (
             "cols xn pp hT z cn cT up trig red nrm tr nm pt es o br mT x1 h2 h2T sh base mask rank more hot tab "
             "idx xT hid y comb h3 out gb step idf oh lo hp half").split()]
        (p_info, p_pos, p_rs, p_rsc, p_rsq, p_prep, p_iota, p_routed, p_gb, p_out, p_step) = [
            sem("p_" + n) for n in "info pos rs rsc rsq prep iota routed gb out step".split()]
        N_SMALL = 8
        PAIRS = TOPK // 2
        LATE = 4
        SPLIT_GATE = 6
        A_GATES, V_GATES = 2 + 2 * KD - SPLIT_GATE, 4 + 2 * KD - SPLIT_GATE
        A_OUT, V_OUT = A_GATES + KD + KD // 2, V_GATES + KD + KD // 2
        COUNTS, TABLE = NT * E, NT * E + 64
        d_pos, d_gmix = sem("d_pos"), sem("d_gmix")

        block = ctx.enter_context(nc.Block())

        def linker(eng, step_sem):
            count = [0]

            def link(ins):
                count[0] += 1
                ins.then_inc(step_sem, 1)
                eng.wait_ge(step_sem, count[0])
            return link

        def tsl(t):
            return slice(t * P, (t + 1) * P)

        units = [(qt, kind, h) for qt in range(NT) for kind in (0, 1) for h in range(8)]

        def band(qt):
            lo, hi = max(0, qt - 1), min(NT - 1, qt + 1)
            return lo, hi - lo + 1

        class Item:
            def __init__(self, it, n, s, uses4, uses2, over=False):
                self.it, self.n, self.s8, self.s4, self.s2 = it, n, s, s % RING, s % 2
                self.uses4, self.uses2 = uses4, uses2
                self.lag2 = 1 if over else 2
                self.lag4 = 1 if over else RING
                self.sc_before = 1 if over else GROUP // 2

        def item(it, s):
            it, s = it + s // GROUP, s % GROUP
            return Item(it, GROUP * it + s, s, (GROUP // RING) * it + s // RING + 1, (GROUP // 2) * it + s // 2 + 1)

        def over_item(j):
            return Item(None, E + j, 0, E // RING + 1 + j, E // 2 + 1 + j, over=True)

        def shift(i, d):
            if isinstance(i.n, int) and not 0 <= i.n + d < E:
                return None
            return item(i.it, i.s8 + d)

        def item_loop(eng, step, first, last):
            lo, hi = -(-first // GROUP), last // GROUP
            for n in range(first, lo * GROUP):
                step(item(0, n))
            with eng.Fori(lo, hi) as it:
                for s in range(GROUP):
                    step(item(it, s))
            for n in range(hi * GROUP, last):
                step(item(0, n))

        def overflow_loop(eng, step):
            eng.wait_ge(v_tab, 3)
            count = eng.value_load(table[0:1, 2, 0:1], min_val=0, max_val=E - 1)
            with eng.If(count > 0):
                with eng.Fori(0, count) as j:
                    step(over_item(j), j)
            eng.end_ifs()

        def h2T_out(act, t):
            act.wait_ge(pe_h2T, 2 * t + 1)
            act.activation(h2T[:, 0:4, tsl(t)], bank[2 * (t % 2)][:].rearrange("p (c q) -> p c q", q=P),
                           ACT.Copy).then_inc(a_h2T, 1)

        def head_out(eng, j):
            eng.wait_ge(pe_tr, j + 1)
            src = bank[j % 4]
            if j < 8:
                dst, src = qT[0:QK, j], src[0:QK, :]
            elif j < 16:
                dst, src = kT[0:QK, j - 8], src[0:QK, :]
            elif j < 20:
                dst, src = qwT[:, j - 16], src[:, :]
            else:
                dst, src = kwT[:, j - 20], src[:, :]
            if j % 2 == 0:
                eng.activation(dst, src, ACT.Copy).then_inc(a_tr, 1)
            else:
                eng.tensor_copy(dst, src).then_inc(v_tr, 1)

        def probT_out(eng, u):
            qt, kind, h = units[u]
            n = T if kind == 0 else band(qt)[1] * P
            eng.wait_ge(pe_t, u + 1)
            if u >= 2:
                eng.wait_ge(pe_pv, u - 1)
            if u % 2 == 0:
                eng.activation(probT[:, 0, 0:n], bank[3][:, 0:n], ACT.Copy).then_inc(a_pt, 1)
            else:
                eng.tensor_copy(probT[:, 1, 0:n], bank[4][:, 0:n]).then_inc(v_pt, 1)

        def pipeline(eng, xT_out, mid, y_out, between=()):
            def step(i):
                if shift(i, -2) is not None:
                    y_out(shift(i, -2))
                mid(i)
                if shift(i, 1) is not None:
                    xT_out(shift(i, 1))
            xT_out(item(0, 0))
            ends = GROUP, E - GROUP
            for n in range(ends[0]):
                step(item(0, n))
                if n < len(between):
                    between[n]()
            item_loop(eng, step, *ends)
            for n in range(ends[1], E):
                step(item(0, n))
            for n in (E - 2, E - 1):
                y_out(item(0, n))

        @block.sync
        def _(sp):
            for t in range(NT):
                sp.dma_start(x_sb[:, t], x[0, tsl(t)]).then_inc(d_x[t], 16)
                if t == 0:
                    sp.dma_start(p_sb, p[0, 0].rearrange("(t p) d -> p t d", p=P)).then_inc(d_p, 16)
                    sp.dma_start(w_pp, w_ple_proj[0].rearrange("(k p) d -> p k d", p=P)).then_inc(d_p, 16)
            for k in range(KD):
                sp.dma_start(w1[:, k], w_in[0, tsl(k), 0:C_GATE]).then_inc(d_w1[k // 2], 16)
            sp.dma_start(wuq, w_uq[0].rearrange("(k p) d -> p k d", p=P)).then_inc(d_wu, 16)
            sp.dma_start(wukv, w_ukv[0].rearrange("(k p) d -> p k d", p=P)).then_inc(d_wu, 16)
            for g in range(KD):
                if g >= 2:
                    sp.wait_ge(pe_g, 2 * (g - 2) + 2)
                c0 = C_GATE + g * 2 * P
                sp.dma_start(w_g[g % 2], w_in[0, :, c0:c0 + 2 * P].rearrange("(k p) c -> p k c", p=P)).then_inc(d_wg[g % 2], 16)
            sp.wait_ge(pe_tr, 2 * MH)
            sp.dma_start(w_bm, w_br_mla[0].rearrange("(k p) d -> p k d", p=P)).then_inc(d_br, 16)
            sp.wait_ge(p_prep, NT)
            sp.dma_start(w_bs, w_br_swa[0].rearrange("(k p) d -> p k d", p=P)).then_inc(d_br, 16)
            sp.wait_ge(pe_pv, UNITS)
            sp.dma_start(w_o, w_out[0].rearrange("(k p) d -> p k d", p=P)).then_inc(d_wo, 16)
            sp.wait_ge(v_mT, KD)
            sp.dma_start(g_moe_b, g_moe[0].partition_broadcast(P)).then_inc(d_wr, 16)
            sp.dma_start(w_r, w_router[0].rearrange("(k p) d -> p k d", p=P)).then_inc(d_wr, 16)
            sp.dma_start(grp[:, 3, 0:E], router_bias[0].partition_broadcast(P)).then_inc(d_wr, 16)
            sp.dma_start(w_sd, w_sh_down[0].rearrange("(k p) d -> p k d", p=P)).then_inc(d_sd, 16)

            def load_gu(i, e=None):
                e = i.n if e is None else e
                sp.dma_start(w_gu[i.s4], w_exp_gu[0, bass.ds(e, 1)].rearrange("a (k p) f -> p (a k) f", p=P)).then_inc(d_gu[i.s4], 16)

            def load_dn(i, e=None):
                e = i.n if e is None else e
                sp.dma_start(w_dn[i.s4], w_exp_down[0, bass.ds(e, 1)].rearrange("a (k p) f -> p (a k) f", p=P)).then_inc(d_dn[i.s4], 16)

            def store_rows(t):
                sp.wait_ge(v_h2, t + 1)
                sp.dma_start(h_rows[tsl(t)], h2[:, t % 2]).then_inc(d_h2[t % 2], 16)
            for t in range(NT - 1):
                store_rows(t)
            sp.wait_ge(pe_wo, NT)
            sp.dma_start(w_sg, w_sh_gu[0].rearrange("(k p) d -> p k d", p=P)).then_inc(d_sg, 16)
            load_gu(item(0, 0))
            store_rows(NT - 1)
            load_gu(item(0, 1))
            load_gu(item(0, 2))
            for d in d_h2:
                sp.wait_ge(d, 32)
            sp.wait_ge(pe_h2T, 2 * NT)
            sp.wait_ge(a_ss, NT + NT)
            load_dn(item(0, 0))
            load_dn(item(0, 1))
            load_gu(item(0, 3))
            sp.wait_ge(pe_sh, 4)
            load_dn(item(0, 2))
            load_dn(item(0, 3))

            def step(i):
                sp.wait_ge(pe_gu, i.n - i.lag4 + 1)
                load_gu(i)
                sp.wait_ge(pe_dn, i.n - i.lag4 + 1)
                load_dn(i)
            item_loop(sp, step, RING, E)
            sp.wait_ge(pe_gu, E - 1)
            sp.dma_start(w_pg, w_ple_gate[0].rearrange("(k p) d -> p k d", p=P)).then_inc(d_pg, 16)
            sp.wait_ge(pe_sd, 2 + LATE)
            sp.dma_start(g_ple_b, g_ple[0].partition_broadcast(P)).then_inc(d_ple, 16)
            sp.dma_start(b_ple_b, b_ple[0].partition_broadcast(P)).then_inc(d_ple, 16)

            def over(i, j):
                e = sp.value_load(table[0:1, 0, bass.ds(j, 1)], min_val=0, max_val=E - 1)
                sp.wait_ge(pe_dn, i.n)
                load_gu(i, e)
                load_dn(i, e)
            overflow_loop(sp, over)

            sp.wait_ge(p_routed, 1)
            sp.wait_ge(d_pps, 16 * NT)
            for c in range(PAIRS * NT):
                t, j = c // PAIRS, 2 * (c % PAIRS)
                if c >= 4:
                    sp.wait_ge(v_comb, c - 3)
                rows_of = y_rows[t * P * TOPK:(t + 1) * P * TOPK].rearrange("(p j) d -> p j d", j=TOPK)
                sp.dma_start(y_in[c % 4], rows_of[:, j:j + 2]).then_inc(d_y[c % 4], 16)
                if c == PAIRS + 2:
                    sp.dma_start(pp_in, pp_rows.rearrange("(t p) d -> p t d", p=P)).then_inc(d_ppi, 16)
            for t in range(NT - 1):
                sp.wait_ge(p_out, t + 1)
                sp.dma_start(out[0, tsl(t)], out_st[:, t % 2]).then_inc(d_out[t % 2], 16)
            for hf in range(2):
                sl = slice(hf * BANK, (hf + 1) * BANK)
                sp.wait_ge(v_out, hf + 1)
                sp.dma_start(out[0, tsl(NT - 1), sl], out_st[:, 1, sl]).then_inc(d_out[1], 16)
            sp.wait_ge(d_out[0], 32)
            sp.wait_ge(d_out[1], 48)

        @block.gpsimd
        def _(pool):
            link = linker(pool, p_step)
            link(pool.memset(ident[:], 0.0))
            link(pool.affine_select(out=ident[:], in_=ident[:], compare_op=ALU.not_equal, fill=1.0, base=0,
                                    pattern=[[-1, P]], channel_multiplier=1))
            pool.tensor_copy(ident_b[:], ident[:])
            pool.memset(half[:], -0.5)
            link(pool.memset(ones_b[:], 1.0))
            pool.affine_select(out=before_b[:], in_=ones_b[:], compare_op=ALU.is_gt, fill=0.0, base=0,
                               pattern=[[1, P]], channel_multiplier=-1)
            link(pool.memset(band_b[:], 0.0))
            pool.affine_select(out=band_b[:, 0], in_=band_b[:, 0], compare_op=ALU.is_ge, fill=NEG, base=0,
                               pattern=[[1, P]], channel_multiplier=-1)
            link(pool.affine_select(out=band_b[:, 1], in_=band_b[:, 1], compare_op=ALU.is_ge, fill=NEG, base=0,
                                    pattern=[[-1, P]], channel_multiplier=1))
            pool.wait_ge(d_pos, 32)
            pool.tensor_copy(pos_f[:], pos_i[:]).then_inc(p_pos, 1)

            def rms(dst, src, n, tmp):
                link(pool.tensor_scalar(tmp, src, 1.0 / n, EPS, ALU.mult, ALU.add))
                return pool.tensor_tensor(dst, tmp, half[:, 0:tmp.shape[1]], ALU.pow)

            for t in range(NT):
                pool.wait_ge(a_ss, t + 1)
                rms(rs[:, t:t + 1], ssum[:, t:t + 1], D, rtmp[:, t:t + 1]).then_inc(p_rs, 1)
            for t in range(NT):
                pool.wait_ge(a_c, t + 1)
                link(rms(rs[:, 8 + 2 * t:9 + 2 * t], ssum[:, 8 + 2 * t:9 + 2 * t], Q_RANK, rtmp[:, 8 + 2 * t:9 + 2 * t]))
                rms(rs[:, 9 + 2 * t:10 + 2 * t], ssum[:, 9 + 2 * t:10 + 2 * t], KV_RANK, rtmp[:, 9 + 2 * t:10 + 2 * t]).then_inc(p_rsc, 1)

            pool.wait_ge(a_trig, 2)
            pool.wait_ge(d_small, 16 * N_SMALL)
            pool.wait_ge(v_cn, NT)
            pool.wait_ge(pe_cT, NT)
            pool.wait_ge(p_rsc, NT)
            link(pool.tensor_scalar(g_q[:], g_q[:], QK ** -0.5, None, ALU.mult))
            link(pool.tensor_scalar(g_s[:, 0], g_s[:, 0], HD ** -0.5, None, ALU.mult))

            def head_scales(t):
                sums, rq = ssq[:, t % 2], rsq[:, t % 2]
                pool.wait_ge(v_red, t + 1)
                link(rms(rq[:, 0:16], sums[:, 0:16], QK, rtmp[:, 0:16]))
                rms(rq[:, 16:26], sums[:, 16:26], HD, rtmp[:, 16:26]).then_inc(p_rsq, 1)
                pool.wait_ge(p_rsq, t + 1)

            head_scales(0)
            for t in range(NT):
                if t + 1 < NT:
                    head_scales(t + 1)
                pool.wait_ge(v_nrm, t + 1)
                if t:
                    pool.wait_ge(p_prep, t)
                qh = q_sb[:, t].rearrange("p (h d) -> p h d", d=QK)
                wh = z[:, t, C_QS:C_VS].rearrange("p (h d) -> p h d", d=HD)

                def rotate(v, heads, nf, f0):
                    x1, x2 = v[:, :, 0:nf], v[:, :, nf:2 * nf]
                    cos = cs[:, 0, t, f0:f0 + nf].unsqueeze(1).broadcast_to([P, heads, nf])
                    sin = cs[:, 1, t, f0:f0 + nf].unsqueeze(1).broadcast_to([P, heads, nf])
                    tmp = [rope_t[:, i, 0:heads * nf].rearrange("p (h d) -> p h d", d=nf) for i in range(4)]
                    pool.tensor_tensor(tmp[0], x1, cos, ALU.mult)
                    pool.tensor_tensor(tmp[1], x2, sin, ALU.mult)
                    pool.tensor_tensor(tmp[2], x2, cos, ALU.mult)
                    link(pool.tensor_tensor(tmp[3], x1, sin, ALU.mult))
                    pool.tensor_tensor(x1, tmp[0], tmp[1], ALU.subtract)
                    link(pool.tensor_tensor(x2, tmp[2], tmp[3], ALU.add))
                rotate(qh[:, :, NOPE:QK], MH, F_M, 0)
                rotate(wh, WH + WKV, F_S, F_M)
                kd = k_dup[:, t].rearrange("p (g c d) -> p g c d", c=2, d=HD)
                pool.tensor_copy(kd[:, :, 0], wh[:, WH:])
                pool.tensor_copy(kd[:, :, 1], wh[:, WH:]).then_inc(p_prep, 1)

            pool.wait_ge(p_prep, NT)
            for t in range(NT):
                pool.wait_ge(a_ss, NT + t + 1)
                rms(rs[:, t:t + 1], ssum[:, t:t + 1], D, rtmp[:, t:t + 1]).then_inc(p_rs, 1)

            pool.wait_ge(v_mT, KD)
            iv = info.rearrange("p e a c -> p c a e")
            link(pool.iota(iot_i[:, 0:2], pattern=[[0, 2]], base=0, channel_multiplier=1))
            link(pool.tensor_copy(tcol[:, 0:1], iot_i[:, 0:1]))
            link(pool.tensor_scalar(tcol[:, 1:2], tcol[:, 0:1], float(TOPK), None, ALU.mult))
            link(pool.memset(info, 0.0))
            pool.tensor_copy(iv[:, 0], tcol[:, 0:1].unsqueeze(2).broadcast_to([P, NT, E]))
            pool.tensor_copy(iv[:, 4], tcol[:, 1:2].unsqueeze(2).broadcast_to([P, NT, E]))
            for a in range(NT):
                pool.memset(iv[:, 1, a], float(P * a))
                pool.memset(iv[:, 5, a], float(TOPK * P * a))
            pool.memset(iv[:, 3], -NO_ROW)
            pool.memset(iv[:, 7], -NO_ROW).then_inc(p_info, 1)
            link(pool.iota(iot_i[:], pattern=[[1, TILES_MAX * SLOTS]], base=0, channel_multiplier=0))
            pool.memset(xg[0], 0.0)
            pool.memset(xg[1], 0.0)
            pool.wait_ge(v_sh, 1)
            pool.tensor_copy(iota, iot_i[:]).then_inc(p_iota, 1)

            last_h, last_y = pool.to_reg(T - 1), pool.to_reg(T * TOPK - 1)

            def held(n):
                return n if isinstance(n, int) else pool.to_reg(n)

            def gather(i, cleared=1):
                first = isinstance(i.n, int) and i.n < RING
                index_due = held(i.n + 1)
                turn_due = None if first else held(i.n - i.lag4 + 1)
                pool.wait_ge(p_iota, cleared)
                pool.wait_ge(v_idx, index_due)
                if not first:
                    pool.wait_ge(pe_T, turn_due)
                pool.indirect_dma_start(xg[i.s4][0:SLOTS], None, h_rows, bass.IndirectOffsetOnAxis(idx[:, i.s8, 0:1], 0),
                                        bounds_check=last_h, oob_is_err=False).then_inc(d_xg[i.s4], 16)

            def scatter(i):
                y_due = held(i.n + 1)
                pool.wait_ge(p_iota, 1)
                pool.wait_ge(a_y, y_due)
                pool.wait_ge(v_y, y_due)
                pool.indirect_dma_start(y_rows, bass.IndirectOffsetOnAxis(idx[:, i.s8, 1:2], 0), y_sb[0:SLOTS, i.s2], None,
                                        bounds_check=last_y, oob_is_err=False).then_inc(d_sc[i.s2], 16)

            pool.wait_ge(d_h2[0], 32)
            pool.wait_ge(d_h2[1], 32)
            gather(item(0, 0))
            gather(item(0, 1))
            pool.wait_ge(v_rank, 2)
            pool.memset(xg[2], 0.0)
            pool.memset(xg[3], 0.0).then_inc(p_iota, 1)
            gather(item(0, 2), 2)

            def step(i):
                if shift(i, -2) is not None:
                    scatter(shift(i, -2))
                if shift(i, 3) is not None:
                    gather(shift(i, 3), 2)
            for n in range(GROUP):
                step(item(0, n))
            item_loop(pool, step, GROUP, E - GROUP)
            for n in range(E - GROUP, E):
                step(item(0, n))
            scatter(item(0, E - 2))
            scatter(item(0, E - 1))
            pool.wait_ge(d_sc[0], 16 * (E // 2))
            pool.wait_ge(d_sc[1], 16 * (E // 2))

            def over(i, j):
                gather(i)
                scatter(i)
                pool.wait_ge(d_sc[0], 16 * i.uses2)
            overflow_loop(pool, over)
            pool.memset(half[:], -0.5).then_inc(p_routed, 1)

            pool.wait_ge(p_routed, 1)

            def tail_out(t):
                pool.wait_ge(a_pg, 2 * t + 2)
                pool.wait_ge(d_ple, 32)
                pool.tensor_tensor(gate3[:, t % 2], gate3[:, t % 2], b_ple_b, ALU.add).then_inc(p_gb, 1)
                pool.wait_ge(a_gate, t + 1)
                pool.wait_ge(d_ppi, 16)
                if t >= 2:
                    pool.wait_ge(d_out[t % 2], 16 * (t // 2))
                link(pool.tensor_tensor(out_st[:, t % 2], gate3[:, t % 2], pp_in[:, t], ALU.mult))
                pool.tensor_tensor(out_st[:, t % 2], out_st[:, t % 2], x_sb[:, t], ALU.add).then_inc(p_out, 1)

            for t in range(NT):
                pool.wait_ge(a_ss, 2 * NT + t + 1)
                rms(rs[:, t:t + 1], ssum[:, t:t + 1], D, rtmp[:, t:t + 1]).then_inc(p_rs, 1)
                if t >= 1:
                    tail_out(t - 1)

        @block.scalar
        def _(act):
            act.dma_start(pos_i[:], positions[0].rearrange("(t p) -> t p", p=P)).then_inc(d_pos, 16)
            act.dma_start(rows[:], b_gate[0].rearrange("(t p) -> t p", p=P)).then_inc(d_pos, 16)
            act.dma_start(g_mix_b, g_mix[0].partition_broadcast(P)).then_inc(d_gmix, 16)
            for dst, src in ((g_cq_b, g_cq), (g_ckv_b, g_ckv), (g_q[:], g_qn_mla), (g_k[:], g_kn_mla),
                             (g_s[:, 0], g_qn_swa), (g_s[:, 1], g_kn_swa), (sink_b[:], sink), (freq[:], rope_freq)):
                act.dma_start(dst, src[0].partition_broadcast(P)).then_inc(d_small, 16)

            def x_squares(t):
                act.wait_ge(d_x[t], 16)
                if t:
                    act.wait_ge(a_ss, t)
                act.activation(z[:, 0, 0:D], x_sb[:, t], ACT.Square, accum_out=ssum[:, t:t + 1]).then_inc(a_ss, 1)

            x_squares(0)
            for t in range(NT):
                act.wait_ge(pe_pT, t + 1)
                act.activation(pT[:, :, tsl(t)], bank[4 + t][:, 0:2 * P].rearrange("p (c q) -> p c q", q=P),
                               ACT.Copy).then_inc(a_pT, 1)
            for t in range(1, NT):
                x_squares(t)
            for t in range(NT):
                act.wait_ge(pe_pp, t + 1)
                act.activation(pp_st[:, t, 0:BANK], bank[2 * (t % 2)][:], ACT.Copy).then_inc(a_pp, 1)
                act.wait_ge(a_pp, t + 1)
                act.wait_ge(v_pp, t + 1)
                act.dma_start(pp_rows[tsl(t)], pp_st[:, t]).then_inc(d_pps, 16)
            for t in range(NT):
                act.wait_ge(pe_hT, 2 * t + 1)
                act.activation(hT[:, 0:4, tsl(t)], bank[4 + 2 * (t % 2)][:].rearrange("p (c q) -> p c q", q=P),
                               ACT.Copy).then_inc(a_hT, 1)

            for c in (0, 1):
                act.wait_ge(v_trig, 1)
                act.activation(cs[:, 1 - c].rearrange("p t f -> p (t f)"), ang[:, 4 + c], ACT.Sin).then_inc(a_trig, 1)

            def z_out(t):
                act.wait_ge(pe_z, t + 1)
                for c in (0, 2):
                    ins = act.activation(z[:, t, c * Z_CHUNK:(c + 1) * Z_CHUNK], bank[3 * (t % 2) + c][:, 0:Z_CHUNK], ACT.Copy)
                    ins.then_inc(a_z, 1)
                act.wait_ge(a_z, 2 * t + 2)
                act.wait_ge(v_z, t + 1)
                if t:
                    act.wait_ge(a_c, t)
                act.activation(sq[:, 0:Q_RANK], z[:, t, 0:Q_RANK], ACT.Square, accum_out=ssum[:, 8 + 2 * t:9 + 2 * t])
                act.activation(sq[:, Q_RANK:C_KR], z[:, t, Q_RANK:C_KR], ACT.Square,
                               accum_out=ssum[:, 9 + 2 * t:10 + 2 * t]).then_inc(a_c, 1)

            def cT_out(t):
                act.wait_ge(pe_cT, t + 1)
                act.activation(cT[:, 0:4, tsl(t)], bank[6][:].rearrange("p (c q) -> p c q", q=P), ACT.Copy).then_inc(a_cT, 1)

            def up_out(t):
                act.wait_ge(pe_up, t + 1)
                half_q, half_kv = MH * QK // 2, MH * (NOPE + VD) // 2
                act.activation(q_sb[:, t, 0:half_q], bank[0][:, 0:half_q], ACT.Copy).then_inc(a_up, 1)
                act.activation(kv[:, t, 0:half_kv], bank[2][:], ACT.Copy).then_inc(a_up, 1)

            def gate_out(c):
                act.wait_ge(pe_g, c + 1)
                act.activation(gT[:, c], bank[4 + c % 2][:], ACT.Sigmoid, bias=cols[:, c:c + 1]).then_inc(a_g, 1)

            def squares(t):
                act.wait_ge(a_up, 2 * t + 2)
                act.wait_ge(v_up, 2 * t + 2)
                act.wait_ge(a_c, NT)
                if t:
                    act.wait_ge(v_red, t)
                act.activation(sq[:, 0:768], q_sb[:, t], ACT.Square)
                act.activation(sq[:, 768:1280].rearrange("p (h d) -> p h d", d=NOPE),
                               kv[:, t].rearrange("p (h d) -> p h d", d=NOPE + VD)[:, :, 0:NOPE], ACT.Square)
                act.activation(sq[:, 1280:1952], z[:, t, C_KR:C_VS], ACT.Square).then_inc(a_sq, 1)

            z_out(0); z_out(1); cT_out(0); z_out(2); cT_out(1); z_out(3); cT_out(2)
            act.wait_ge(v_cols, 1)
            act.wait_ge(d_pps, 16 * NT)
            gate_out(0)
            cT_out(3)
            for t in range(NT):
                up_out(t)
                gate_out(t + 1) if t < 3 else None

            def gate_upper(c):
                g = c // 2
                act.wait_ge(d_wg[g % 2], 16 * (g // 2 + 1))
                if c >= SPLIT_GATE + 2:
                    act.wait_ge(pe_g, c - 1)
                act.activation(wg_hi[c % 2], w_g[g % 2][:, :, (c % 2) * P:(c % 2 + 1) * P], ACT.Copy).then_inc(a_half, 1)

            squares(0)
            act.wait_ge(pe_up, NT)
            act.wait_ge(v_hT, NT)
            for i in range(2):
                act.activation(h_hi[i], hT[:, 4 * i:4 * i + 4], ACT.Copy).then_inc(a_half, 1)
            squares(1)
            gate_upper(6); gate_out(4)
            squares(2)
            gate_upper(7); gate_out(5)
            for c in range(SPLIT_GATE, 2 * KD):
                gate_out(c)
                if c + 2 < 2 * KD:
                    gate_upper(c + 2)
                if c == SPLIT_GATE + 1:
                    squares(3)

            for j in range(0, 22, 2):
                head_out(act, j)

            act.wait_ge(d_small, 16 * N_SMALL)
            last = UNITS - 1
            for i in range(UNITS + 16):
                if i < UNITS:
                    qt, kind, h = units[i]
                    n = T if kind == 0 else band(qt)[1] * P
                    act.wait_ge(v_nm, i + 1)
                    act.wait_ge(pe_s, i + 1)
                    if i >= 2:
                        act.wait_ge(pe_t, i - 1)
                    act.activation(prob[:, i % 2, 0:n], bank[i % 3][:, 0:n], ACT.Exp, bias=nmax[:, i:i + 1],
                                   accum_out=lsum[:, i:i + 1]).then_inc(a_e, 1)
                if 0 <= i - 2 < UNITS and i % 2 == 0:
                    probT_out(act, i - 2)
                if i >= 10 and (i - 10) % 16 == 8:
                    g = (i - 10) // 8
                    act.wait_ge(v_es, (g + 1) // 2)
                    act.activation(es[:, 0:WH], es[:, WH:2 * WH], ACT.Exp).then_inc(a_es, 1)
                if i >= 13 and (i - 13) % 8 == 0 and (i - 13) // 8 < 2 * NT:
                    g = (i - 13) // 8
                    act.wait_ge(pe_ot, g + 1)
                    dst = (oT_m, oT_w)[g % 2]
                    act.activation(dst[:, :, tsl(g // 2)], bank[7][:].rearrange("p (c q) -> p c q", q=P),
                                   ACT.Copy).then_inc(a_oT, 1)

            act.wait_ge(d_wo, 16)
            act.wait_ge(pe_pv, UNITS)
            for c in range(KD):
                if c < KD // 2:
                    act.activation(wo_hi[c], w_o[:, 2 * c:2 * c + 2], ACT.Copy).then_inc(a_half, 1)
                act.wait_ge(v_mT, c + 1)
                act.activation(m_hi[c], mT[:, c], ACT.Copy).then_inc(a_half, 1)

            for t in range(NT):
                act.wait_ge(v_x1, 2 * t + 2)
                if t:
                    act.wait_ge(a_ss, NT + t)
                act.activation(junk2, x_sb[:, t], ACT.Square, accum_out=ssum[:, t:t + 1]).then_inc(a_ss, 1)
                if t >= 1:
                    h2T_out(act, t - 1)
            h2T_out(act, NT - 1)
            act.wait_ge(pe_lg, 1)
            act.activation(rt[0].rearrange("p a e -> p (a e)"), bank[4][:, 0:NT * E], ACT.Sigmoid).then_inc(a_sc, 1)
            for c in range(2):
                act.wait_ge(pe_sh, c + 1)
                act.activation(shT[:, c], bank[5 + c][:], ACT.Silu).then_inc(a_ssh, 1)

            def xT_out(i):
                act.wait_ge(pe_T, i.n + 1)
                if not (isinstance(i.n, int) and i.n < 2):
                    act.wait_ge(pe_gu, i.n - i.lag2 + 1)
                act.activation(xT[:, i.s2, 0:4], bank[0][:, 0:4 * SLOTS].rearrange("p (k s) -> p k s", s=SLOTS),
                               ACT.Copy).then_inc(a_xT, 1)

            def silu(i):
                act.wait_ge(d_dn[i.s4], 16 * i.uses4)
                if not (isinstance(i.n, int) and i.n < 2):
                    act.wait_ge(pe_dn, i.n - i.lag2 + 1)
                act.activation(w_hi[i.s2], w_dn[i.s4], ACT.Copy).then_inc(a_hi, 1)
                act.wait_ge(pe_gu, i.n + 1)
                if not (isinstance(i.n, int) and i.n < 2):
                    act.wait_ge(v_hid, i.n - i.lag2 + 1)
                act.activation(sg[:, i.s2], bank[2 + i.s2][:, 0:2 * SLOTS].rearrange("p (c s) -> p c s", s=SLOTS),
                               ACT.Silu).then_inc(a_sg, 1)

            def y_out(i):
                act.wait_ge(pe_dn, i.n + 1)
                if not (isinstance(i.n, int) and i.n < 2):
                    act.wait_ge(d_sc[i.s2], 16 * (i.uses2 - 1))
                act.activation(y_sb[0:SLOTS, i.s2, 0:BANK], bank[4][0:SLOTS, :], ACT.Copy).then_inc(a_y, 1)

            act.wait_ge(pe_sh, 4)
            pipeline(act, xT_out, silu, y_out)

            def over(i, j):
                xT_out(i)
                silu(i)
                y_out(i)
            overflow_loop(act, over)

            act.wait_ge(d_pg, 16)
            act.wait_ge(pe_gu, E)
            act.wait_ge(pe_dn, E - 1)
            for i in range(KD // 2):
                act.activation(pg_hi[i], w_pg[:, 2 * i:2 * i + 2], ACT.Copy).then_inc(a_half, 1)

            def gate_part(t):
                for hf in range(2):
                    act.wait_ge(pe_pg, 2 * t + hf + 1)
                    if t >= 2:
                        act.wait_ge(p_out, t - 1)
                    act.activation(gate3[:, t % 2, hf * BANK:(hf + 1) * BANK], bank[4 + 2 * (t % 2) + hf][:], ACT.Copy).then_inc(a_pg, 1)
                act.wait_ge(p_gb, t + 1)
                act.activation(gate3[:, t % 2], gate3[:, t % 2], ACT.Sigmoid).then_inc(a_gate, 1)

            for t in range(NT):
                act.wait_ge(v_comb, PAIRS * (t + 1))
                act.wait_ge(a_ss, 2 * NT + t) if t else act.wait_ge(p_routed, 1)
                act.activation(junk3, x_sb[:, t], ACT.Square, accum_out=ssum[:, t:t + 1]).then_inc(a_ss, 1)
                for hf in range(2):
                    act.wait_ge(pe_h3T, 2 * t + hf + 1)
                    if t >= 2:
                        act.wait_ge(pe_pg, 2 * t - 2)
                    act.activation(h3_hi[t % 2][:, 4 * hf:4 * hf + 4], bank[2 * (t % 2) + hf][:].rearrange("p (c q) -> p c q", q=P),
                                   ACT.Copy).then_inc(a_h3T, 1)
                if 1 <= t:
                    gate_part(t - 1)
            for hf in range(2):
                act.wait_ge(v_gb, hf + 1)
                sl = slice(hf * BANK, (hf + 1) * BANK)
                act.activation(gate3[:, 1, sl], gate3[:, 1, sl], ACT.Sigmoid).then_inc(a_gate, 1)

        @block.vector
        def _(dve):
            link = linker(dve, v_step)
            dve.wait_ge(pe_rows, 1)
            dve.tensor_copy(cols[:], bank[7][:, 0:2 * KD + NT]).then_inc(v_cols, 1)
            dve.wait_ge(d_gmix, 16)

            def xn_tile(t):
                dve.wait_ge(p_rs, t + 1)
                dve.wait_ge(d_x[t], 16)
                if t >= 2:
                    dve.wait_ge(pe_hT, 2 * (t - 2) + 2)
                dve.scalar_tensor_tensor(xn[:, t % 2], x_sb[:, t], rs[:, t:t + 1], g_mix_b, ALU.mult, ALU.mult).then_inc(v_xn, 1)

            def hT_tile(t):
                dve.wait_ge(pe_hT, 2 * t + 2)
                dve.tensor_copy(hT[:, 4:8, tsl(t)], bank[5 + 2 * (t % 2)][:].rearrange("p (c q) -> p c q", q=P)).then_inc(v_hT, 1)

            xn_tile(0); xn_tile(1)
            for t in range(NT):
                dve.wait_ge(pe_pp, t + 1)
                dve.tensor_copy(pp_st[:, t, BANK:D], bank[2 * (t % 2) + 1][:]).then_inc(v_pp, 1)
            hT_tile(0); xn_tile(2); hT_tile(1); xn_tile(3); hT_tile(2); hT_tile(3)

            dve.wait_ge(d_small, 16 * N_SMALL)
            a, turns, r0, r1, r, rc = (ang[:, i] for i in range(6))
            for t in range(NT):
                ins = dve.tensor_scalar(a[:, t * NF:(t + 1) * NF], freq[:], cols[:, 2 * KD + t:2 * KD + t + 1], None, ALU.mult)
            link(ins)
            link(dve.tensor_scalar(turns, a, 1.0 / (2 * math.pi), ROUND, ALU.mult, ALU.add))
            link(dve.tensor_scalar(turns, turns, ROUND, None, ALU.subtract))
            link(dve.scalar_tensor_tensor(r0, turns, -TWO_PI[0], a, ALU.mult, ALU.add))
            link(dve.scalar_tensor_tensor(r1, turns, -TWO_PI[1], r0, ALU.mult, ALU.add))
            link(dve.scalar_tensor_tensor(r0, turns, -TWO_PI[2], r1, ALU.mult, ALU.add))
            link(dve.tensor_scalar(r, r0, 3.1415925, -3.1415925, ALU.min, ALU.max))
            link(dve.scalar_tensor_tensor(r1, r, -1.0, r, ALU.mult, ALU.max))
            dve.tensor_scalar(rc, r1, -1.0, math.pi / 2, ALU.mult, ALU.add).then_inc(v_trig, 1)

            def z_tile(t):
                dve.wait_ge(pe_z, t + 1)
                dve.wait_ge(a_ss, NT)
                dve.tensor_copy(z[:, t, Z_CHUNK:2 * Z_CHUNK], bank[3 * (t % 2) + 1][:, 0:Z_CHUNK]).then_inc(v_z, 1)
                dve.wait_ge(a_z, 2 * t + 2)
                dve.wait_ge(v_z, t + 1)
                dve.wait_ge(p_rsc, t + 1)
                if t >= 2:
                    dve.wait_ge(pe_cT, t - 1)
                dve.scalar_tensor_tensor(c_n[:, t % 2, 0:Q_RANK], z[:, t, 0:Q_RANK], rs[:, 8 + 2 * t:9 + 2 * t],
                                         g_cq_b, ALU.mult, ALU.mult)
                dve.scalar_tensor_tensor(c_n[:, t % 2, Q_RANK:C_KR], z[:, t, Q_RANK:C_KR], rs[:, 9 + 2 * t:10 + 2 * t],
                                         g_ckv_b, ALU.mult, ALU.mult).then_inc(v_cn, 1)

            def cT_tile(t):
                dve.wait_ge(pe_cT, t + 1)
                dve.tensor_copy(cT[:, 4, tsl(t)], bank[7][:, 0:P]).then_inc(v_cT, 1)

            z_tile(0); z_tile(1); cT_tile(0); z_tile(2); cT_tile(1); z_tile(3); cT_tile(2); cT_tile(3)
            half_q, half_kv = MH * QK // 2, MH * (NOPE + VD) // 2
            for t in range(NT):
                dve.wait_ge(pe_up, t + 1)
                dve.tensor_copy(q_sb[:, t, half_q:], bank[1][:, 0:half_q]).then_inc(v_up, 1)
                dve.tensor_copy(kv[:, t, half_kv:], bank[3][:]).then_inc(v_up, 1)

            def head_sums(t):
                dve.wait_ge(a_sq, t + 1)
                if t >= 2:
                    dve.wait_ge(p_rsq, t - 1)
                sums = ssq[:, t % 2]
                dve.tensor_reduce(sums[:, 0:8], sq[:, 0:768].rearrange("p (h d) -> p h d", d=QK), AX.X, ALU.add)
                dve.tensor_reduce(sums[:, 8:16], sq[:, 768:1280].rearrange("p (h d) -> p h d", d=NOPE), AX.X, ALU.add)
                dve.tensor_reduce(sums[:, 26:27], sq[:, 1280:1312], AX.X, ALU.add)
                link(dve.tensor_reduce(sums[:, 16:26], sq[:, 1312:1952].rearrange("p (h d) -> p h d", d=HD), AX.X, ALU.add))
                dve.tensor_scalar(sums[:, 8:16], sums[:, 8:16], sums[:, 26:27], None, ALU.add).then_inc(v_red, 1)

            def head_norms(t):
                dve.wait_ge(p_rsq, t + 1)
                dve.wait_ge(v_red, t + 1)
                if t:
                    dve.wait_ge(v_nrm, t)
                rq = rsq[:, t % 2]
                qh = q_sb[:, t].rearrange("p (h d) -> p h d", d=QK)
                kh = kk[:, t].rearrange("p (h d) -> p h d", d=QK)
                kvh = kv[:, t].rearrange("p (h d) -> p h d", d=NOPE + VD)
                wh = z[:, t, C_QS:C_VS].rearrange("p (h d) -> p h d", d=HD)
                dve.tensor_tensor(qh, qh, rq[:, 0:8].unsqueeze(2).broadcast_to([P, MH, QK]), ALU.mult)
                dve.tensor_tensor(kh[:, :, 0:NOPE], kvh[:, :, 0:NOPE], rq[:, 8:16].unsqueeze(2).broadcast_to([P, MH, NOPE]), ALU.mult)
                dve.tensor_tensor(wh, wh, rq[:, 16:26].unsqueeze(2).broadcast_to([P, WH + WKV, HD]), ALU.mult)
                krg = kr_t[:, 0:2]
                link(dve.tensor_tensor(krg.rearrange("p a f -> p (a f)"), z[:, t, C_KR:C_QS], g_k[:, NOPE:QK], ALU.mult))
                cos, sin = cs[:, 0, t, 0:F_M], cs[:, 1, t, 0:F_M]
                dve.tensor_tensor(kr_t[:, 2], krg[:, 0], cos, ALU.mult)
                dve.tensor_tensor(kr_t[:, 3], krg[:, 1], sin, ALU.mult)
                dve.tensor_tensor(kr_t[:, 4], krg[:, 1], cos, ALU.mult)
                link(dve.tensor_tensor(kr_t[:, 5], krg[:, 0], sin, ALU.mult))
                dve.tensor_tensor(krg[:, 0], kr_t[:, 2], kr_t[:, 3], ALU.subtract)
                link(dve.tensor_tensor(krg[:, 1], kr_t[:, 4], kr_t[:, 5], ALU.add))
                dve.tensor_tensor(kh[:, :, NOPE:QK], krg.rearrange("p a f -> p (a f)").unsqueeze(1).broadcast_to([P, MH, ROPE]),
                                  rq[:, 8:16].unsqueeze(2).broadcast_to([P, MH, ROPE]), ALU.mult)
                dve.tensor_tensor(qh, qh, g_q[:, 0:QK].unsqueeze(1).broadcast_to([P, MH, QK]), ALU.mult)
                dve.tensor_tensor(kh[:, :, 0:NOPE], kh[:, :, 0:NOPE], g_k[:, 0:NOPE].unsqueeze(1).broadcast_to([P, MH, NOPE]), ALU.mult)
                dve.tensor_tensor(wh[:, 0:WH], wh[:, 0:WH], g_s[:, 0].unsqueeze(1).broadcast_to([P, WH, HD]), ALU.mult)
                dve.tensor_tensor(wh[:, WH:], wh[:, WH:], g_s[:, 1].unsqueeze(1).broadcast_to([P, WKV, HD]), ALU.mult).then_inc(v_nrm, 1)

            def rows_lower(part, k0, n, src):
                dve.tensor_tensor(part, hT[:, k0:k0 + n], src.bitcast(f32), ALU.subtract).then_inc(v_half, 1)

            def gate_lower(c):
                g, cols_of = c // 2, slice((c % 2) * P, (c % 2 + 1) * P)
                dve.wait_ge(a_half, 2 + c - SPLIT_GATE + 1)
                dve.wait_ge(d_wg[g % 2], 16 * (g // 2 + 1))
                dve.tensor_tensor(wg_lo[g % 2][:, :, cols_of], w_g[g % 2][:, :, cols_of], wg_hi[c % 2].bitcast(f32),
                                  ALU.subtract).then_inc(v_half, 1)

            dve.wait_ge(a_trig, 2)
            head_sums(0)
            dve.wait_ge(a_hT, NT)
            dve.wait_ge(a_half, 2)
            rows_lower(h_lo[0], 0, 3, h_hi[0][:, 0:3])
            rows_lower(h_lo[1][:, 0:1], 3, 1, h_hi[0][:, 3:4])
            rows_lower(h_lo[1][:, 1:2], 4, 1, h_hi[1][:, 0:1])
            head_sums(1)
            gate_lower(6); gate_lower(7)
            dve.wait_ge(pe_g, SPLIT_GATE)
            rows_lower(h_lo[2], 5, 3, h_hi[1][:, 1:4])
            head_norms(0)
            gate_lower(8)
            head_sums(2)
            gate_lower(9)
            head_norms(1)
            gate_lower(10)
            head_sums(3)
            gate_lower(11)
            head_norms(2)
            gate_lower(12); gate_lower(13)
            head_norms(3)
            gate_lower(14); gate_lower(15)

            for j in range(1, 22, 2):
                head_out(dve, j)

            def group_out(g):
                qt, kind = g // 2, g % 2
                dve.wait_ge(pe_pv, 8 * g + 8)
                dve.wait_ge(a_e, 8 * g + 8)
                ls = lsum[:, 8 * g:8 * g + 8]
                if kind:
                    dve.wait_ge(a_es, qt + 1)
                    link(dve.tensor_tensor(ls, ls, es[:, 0:WH], ALU.add))
                link(dve.reciprocal(ls, ls))
                if g:
                    dve.wait_ge(pe_ot, g)
                dve.tensor_tensor(o_sb.rearrange("p (h d) -> p h d", d=VD), bank[5 + g % 2][:].rearrange("p (h d) -> p h d", d=VD),
                                  ls.unsqueeze(2).broadcast_to([P, 8, VD]), ALU.mult).then_inc(v_o, 1)

            for i in range(UNITS + 16):
                if i < UNITS:
                    qt, kind, h = units[i]
                    n = T if kind == 0 else band(qt)[1] * P
                    dve.wait_ge(pe_s, i + 1)
                    if kind == 0:
                        dve.tensor_reduce(nmax[:, i:i + 1], bank[i % 3][:, 0:n], AX.X, ALU.max, negate=True).then_inc(v_nm, 1)
                    else:
                        link(dve.tensor_reduce(mx1[:, i % 2:i % 2 + 1], bank[i % 3][:, 0:n], AX.X, ALU.max))
                        dve.tensor_scalar(nmax[:, i:i + 1], mx1[:, i % 2:i % 2 + 1], sink_b[:, h:h + 1], -1.0, ALU.max, ALU.mult).then_inc(v_nm, 1)
                if 0 <= i - 2 < UNITS and i % 2 == 1:
                    probT_out(dve, i - 2)
                if i >= 9 and (i - 9) % 16 == 8 and (i - 9) // 8 < 2 * NT:
                    g = (i - 9) // 8
                    dve.wait_ge(v_nm, 8 * g + 8)
                    if g > 1:
                        dve.wait_ge(a_es, g // 2)
                    dve.tensor_tensor(es[:, WH:2 * WH], sink_b[:], nmax[:, 8 * g:8 * g + 8], ALU.add).then_inc(v_es, 1)
                if i >= 11 and (i - 11) % 8 == 0 and (i - 11) // 8 < 2 * NT:
                    group_out((i - 11) // 8)

            def lower_merged(c):
                dve.wait_ge(a_half, A_GATES + min(2 * c + 2, c + 1 + KD // 2))
                dve.tensor_tensor(m_lo[c], mT[:, c], m_hi[c].bitcast(f32), ALU.subtract).then_inc(v_half, 1)
                if c < KD // 2:
                    dve.wait_ge(d_wo, 16)
                    dve.tensor_tensor(wo_lo[c], w_o[:, 2 * c:2 * c + 2], wo_hi[c].bitcast(f32), ALU.subtract).then_inc(v_half, 1)

            for c in range(KD):
                dve.wait_ge(pe_br, c + 1)
                dve.wait_ge(a_g, 2 * KD)
                if c:
                    dve.wait_ge(v_mT, c)
                dve.tensor_tensor(mT[:, c], bank[c % 2][:], gT[:, c], ALU.mult)
                dve.tensor_tensor(br_t, bank[2 + c % 2][:], gT[:, KD + c], ALU.mult).then_inc(v_br, 1)
                dve.wait_ge(v_br, c + 1)
                dve.tensor_tensor(mT[:, c], mT[:, c], br_t, ALU.add).then_inc(v_mT, 1)
                if c:
                    lower_merged(c - 1)
            dve.wait_ge(v_mT, KD)
            lower_merged(KD - 1)

            def x1_tile(t):
                dve.wait_ge(pe_wo, t + 1)
                for hf in range(2):
                    sl = slice(hf * BANK, (hf + 1) * BANK)
                    dve.tensor_tensor(x_sb[:, t, sl], bank[4 + 2 * (t % 2) + hf][:], x_sb[:, t, sl], ALU.add).then_inc(v_x1, 1)

            def h2_tile(t):
                dve.wait_ge(p_rs, NT + t + 1)
                dve.wait_ge(d_wr, 48)
                dve.wait_ge(v_x1, 2 * t + 2)
                if t >= 2:
                    dve.wait_ge(pe_h2T, 2 * (t - 2) + 2)
                    dve.wait_ge(d_h2[t % 2], 16)
                dve.scalar_tensor_tensor(h2[:, t % 2], x_sb[:, t], rs[:, t:t + 1], g_moe_b, ALU.mult, ALU.mult).then_inc(v_h2, 1)

            def h2T_tile(t):
                dve.wait_ge(pe_h2T, 2 * t + 2)
                dve.tensor_copy(h2T[:, 4:8, tsl(t)], bank[1 + 2 * (t % 2)][:].rearrange("p (c q) -> p c q", q=P)).then_inc(v_h2T, 1)
            x1_tile(0); h2_tile(0); x1_tile(1); h2T_tile(0); h2_tile(1); x1_tile(2); h2T_tile(1); h2_tile(2)
            x1_tile(3); h2T_tile(2); h2_tile(3); h2T_tile(3)

            scores, sel, masked, left, chosen, wn, seen, eq = rt
            bias_v = grp[:, 3, 0:E]
            dve.wait_ge(a_sc, 1)
            link(dve.tensor_tensor(sel, scores, bias_v.unsqueeze(1).broadcast_to([P, NT, E]), ALU.add))
            top = grp[:, 0].rearrange("p (a g k) -> p a g k", g=GROUPS, k=8)
            for a_ in range(NT):
                for g in range(GROUPS):
                    ins = dve.max(top[:, a_, g], sel[:, a_, g * PER_GROUP:(g + 1) * PER_GROUP])
            link(ins)
            gs = grp[:, 3, E:E + NT * GROUPS].rearrange("p (a g) -> p a g", g=GROUPS)
            link(dve.tensor_tensor(gs, top[:, :, :, 0], top[:, :, :, 1], ALU.add))
            pair, pair2 = (grp[:, i].rearrange("p (a g k) -> p a g k", g=GROUPS, k=GROUPS) for i in (1, 2))
            for a_ in range(NT):
                me = gs[:, a_].unsqueeze(2).broadcast_to([P, GROUPS, GROUPS])
                other = gs[:, a_].unsqueeze(1).broadcast_to([P, GROUPS, GROUPS])
                dve.tensor_tensor(pair[:, a_], other, me, ALU.is_gt)
                ins = dve.tensor_tensor(pair2[:, a_], other, me, ALU.is_equal)
            link(ins)
            for g in range(GROUPS - 1):
                for_me = pair2[:, :, g, g:GROUPS] if g else pair2[:, :, 0, 0:GROUPS]
                ins = dve.memset(for_me, 0.0)
            link(dve.memset(pair2[:, :, GROUPS - 1, GROUPS - 1:GROUPS], 0.0))
            link(dve.tensor_tensor(pair, pair, pair2, ALU.add))
            place = grp[:, 3, E + 32:E + 64].rearrange("p (a g) -> p a g", g=GROUPS)
            link(dve.tensor_reduce(place, pair, AX.X, ALU.add))
            link(dve.tensor_scalar(gs, place, float(TOPG), None, ALU.is_lt))
            link(dve.tensor_scalar(place, gs, -NEG, NEG, ALU.mult, ALU.add))
            for a_ in range(NT):
                me = sel[:, a_].rearrange("p (g k) -> p g k", k=PER_GROUP)
                mk = masked[:, a_].rearrange("p (g k) -> p g k", k=PER_GROUP)
                link(dve.tensor_tensor(mk, me, gs[:, a_].unsqueeze(2).broadcast_to([P, GROUPS, PER_GROUP]), ALU.mult))
                link(dve.tensor_tensor(mk, mk, place[:, a_].unsqueeze(2).broadcast_to([P, GROUPS, PER_GROUP]), ALU.add))
            for a_ in range(NT):
                link(dve.max(top[:, 0, a_], masked[:, a_]))
                link(dve.match_replace(left[:, a_], top[:, 0, a_], masked[:, a_], 4 * NEG))
            link(dve.tensor_scalar(chosen, left, 2 * NEG, None, ALU.is_lt))
            link(dve.tensor_copy(mask_b[:], chosen))
            dve.tensor_tensor(wn, scores, chosen, ALU.mult).then_inc(v_mask, 1)
            dve.wait_ge(v_mask, 1)
            tot = grp[:, 3, E:E + NT]
            link(dve.tensor_reduce(tot, wn, AX.X, ALU.add))
            link(dve.reciprocal(tot, tot))
            for a_ in range(NT):
                ins = dve.tensor_scalar(wn[:, a_], wn[:, a_], tot[:, a_:a_ + 1], ROUTED_SCALE, ALU.mult, ALU.mult)
            link(ins)
            link(dve.memset(eq, 1.0))
            for a_ in range(NT):
                ins = dve.tensor_tensor_scan(seen[:, a_], eq[:, a_], chosen[:, a_], 0.0, ALU.mult, ALU.add)
            link(ins)
            for j in range(TOPK):
                link(dve.scalar_tensor_tensor(eq, seen, float(j + 1), wn, ALU.is_equal, ALU.mult))
                link(dve.tensor_reduce(wj[:, :, j:j + 1].rearrange("p a c -> p (a c)"), eq, AX.X, ALU.add))
            for c in range(2):
                dve.wait_ge(pe_sh, 3 + c)
                dve.wait_ge(a_ssh, c + 1)
                dve.tensor_tensor(shT[:, c], bank[(7, 0)[c]][:], shT[:, c], ALU.mult).then_inc(v_sh, 1)
            dve.wait_ge(pe_rank, 1)
            dve.wait_ge(p_info, 1)
            link(dve.scalar_tensor_tensor(rank, bank[6][:, 0:NT * E].rearrange("p (a e) -> p a e", e=E), 1.0, chosen, ALU.add, ALU.mult))
            dve.tensor_scalar(rank, rank, -1.0, None, ALU.add).then_inc(v_rank, 1)
            dve.tensor_scalar(info.rearrange("p e a c -> p c a e")[:, 6], seen, -1.0, None, ALU.add).then_inc(v_rank, 1)

            extra, start = more[:, 0:1], more[:, 1:2]
            hot = [tab_t[0:E, i] for i in range(TILES_MAX - 1)]
            val = tab_t[0:E, TILES_MAX - 1]

            def overflow_counts():
                link(dve.tensor_scalar(extra, bank[6][0:E, COUNTS:COUNTS + 1], float(SLOTS), None, ALU.is_gt))
                for k in range(2, TILES_MAX):
                    link(dve.tensor_scalar(more[:, 3:4], bank[6][0:E, COUNTS:COUNTS + 1], float(SLOTS * k), None, ALU.is_gt))
                    link(dve.tensor_tensor(extra, extra, more[:, 3:4], ALU.add))
                dve.tensor_copy(more_b[:, 0:1], extra).then_inc(v_more, 1)

            def overflow_places():
                dve.wait_ge(pe_st, 1)
                link(dve.tensor_copy(start, bank[6][0:E, COUNTS + 1:COUNTS + 2]))
                for k in range(1, TILES_MAX):
                    link(dve.tensor_scalar(more[:, 4:5], start, float(k - 1), None, ALU.add))
                    link(dve.tensor_scalar(more[:, 5:6], extra, float(k), None, ALU.is_ge))
                    link(dve.tensor_scalar(hot[k - 1], iota[0:E, 0:E], more[:, 4:5], more[:, 5:6], ALU.is_equal, ALU.mult))
                for k in range(1, TILES_MAX):
                    link(dve.memset(val[:, k:k + 1], float(k * SLOTS)))
                dve.tensor_copy(val[:, 0:1], tcol[0:E, 0:1]).then_inc(v_hot, 1)

            def overflow_table():
                dve.wait_ge(pe_tab, 1)
                dve.tensor_copy(table[0:1, 0], bank[6][0:1, TABLE:TABLE + E]).then_inc(v_tab, 1)
                dve.tensor_copy(table[0:1, 1], bank[6][0:1, TABLE + E:TABLE + 2 * E]).then_inc(v_tab, 1)
                dve.tensor_copy(table[0:1, 2, 0:1], bank[6][0:1, COUNTS + 2:COUNTS + 3]).then_inc(v_tab, 1)

            def one_hot(i, e=None, k=0):
                e = i.n if e is None else e
                if not (isinstance(i.n, int) and i.n < 2):
                    dve.wait_ge(pe_info, i.n - i.lag2 + 1)
                dve.tensor_copy(info_t[:, i.s2], info[:, bass.ds(e, 1)].rearrange("p e a c -> p (e a c)"))
                dve.tensor_tensor(
                    onehot[:, i.s2], iota[:, bass.ds(k, SLOTS)].unsqueeze(1).broadcast_to([P, NT, SLOTS]),
                    rank[:, :, bass.ds(e, 1)].broadcast_to([P, NT, SLOTS]), ALU.is_equal).then_inc(v_oh, 1)

            def index(i):
                dve.wait_ge(pe_info, i.n + 1)
                if not (isinstance(i.n, int) and i.n < GROUP):
                    dve.wait_ge(d_sc[i.s2], 16 * (i.uses2 - i.sc_before))
                dve.tensor_reduce(idx_f[:, i.s2], bank[7][0:SLOTS, 0:8].rearrange("p (w c) -> p w c", c=4), AX.X, ALU.add).then_inc(v_idf, 1)
                dve.wait_ge(v_idf, i.n + 1)
                dve.tensor_scalar(idx[:, i.s8], idx_f[:, i.s2], NO_ROW, None, ALU.add).then_inc(v_idx, 1)

            def xT_tile(i):
                dve.wait_ge(pe_T, i.n + 1)
                if not (isinstance(i.n, int) and i.n < 2):
                    dve.wait_ge(pe_gu, i.n - i.lag2 + 1)
                dve.tensor_copy(xT[:, i.s2, 4:8], bank[1][:, 0:4 * SLOTS].rearrange("p (k s) -> p k s", s=SLOTS)).then_inc(v_xT, 1)

            def lower(i):
                dve.wait_ge(a_hi, i.n + 1)
                dve.wait_ge(d_dn[i.s4], 16 * i.uses4)
                dve.tensor_tensor(w_lo[i.s4], w_dn[i.s4], w_hi[i.s2].bitcast(f32), ALU.subtract).then_inc(v_lo, 1)

            def hidden(i):
                dve.wait_ge(a_sg, i.n + 1)
                if not (isinstance(i.n, int) and i.n < 2):
                    dve.wait_ge(pe_dn, i.n - i.lag2 + 1)
                dve.tensor_tensor(hidT[:, i.s2], bank[2 + i.s2][:, 2 * SLOTS:4 * SLOTS].rearrange("p (c s) -> p c s", s=SLOTS),
                                  sg[:, i.s2], ALU.mult).then_inc(v_hp, 1)
                dve.wait_ge(v_hp, 2 * i.n + 1)
                dve.tensor_copy(hid_hi[:, i.s2], hidT[:, i.s2]).then_inc(v_hp, 1)
                dve.wait_ge(v_hp, 2 * i.n + 2)
                dve.tensor_tensor(hid_lo[:, i.s2], hidT[:, i.s2], hid_hi[:, i.s2].bitcast(f32), ALU.subtract).then_inc(v_hid, 1)

            def y_tile(i):
                dve.wait_ge(pe_dn, i.n + 1)
                if not (isinstance(i.n, int) and i.n < 2):
                    dve.wait_ge(d_sc[i.s2], 16 * (i.uses2 - 1))
                dve.tensor_copy(y_sb[0:SLOTS, i.s2, BANK:D], bank[5][0:SLOTS, :]).then_inc(v_y, 1)

            def mid(i):
                n3, n4 = shift(i, 3), shift(i, 4)
                lower(i)
                if n3 is not None:
                    index(n3)
                hidden(i)
                if n4 is not None:
                    one_hot(n4)
            dve.wait_ge(v_rank, 2)
            dve.wait_ge(p_iota, 1)

            def base_tile(t):
                dve.wait_ge(pe_sd, t + 1)
                for hf, b in enumerate(((1, 2), (3, 5))[t]):
                    sl = slice(hf * BANK, (hf + 1) * BANK)
                    dve.tensor_tensor(x_sb[:, t, sl], bank[b][:], x_sb[:, t, sl], ALU.add).then_inc(v_base, 1)

            def late_base(u):
                dve.wait_ge(pe_sd, 2 + u + 1)
                sl = slice((u % 2) * BANK, (u % 2 + 1) * BANK)
                dve.tensor_tensor(x_sb[:, 2 + u // 2, sl], bank[6][:], x_sb[:, 2 + u // 2, sl], ALU.add).then_inc(v_base, 1)

            for n in range(3):
                one_hot(item(0, n))
                if n < 2:
                    base_tile(n)
                index(item(0, n))
            one_hot(item(0, 3))
            pipeline(dve, xT_tile, mid, y_tile, [overflow_counts, overflow_places, overflow_table, lambda: None] +
                     [lambda u=u: late_base(u) for u in range(LATE)])

            def over(i, j):
                e = dve.value_load(table[0:1, 0, bass.ds(j, 1)], min_val=0, max_val=E - 1)
                k = dve.value_load(table[0:1, 1, bass.ds(j, 1)], min_val=0, max_val=(TILES_MAX - 1) * SLOTS)
                one_hot(i, e, k)
                index(i)
                xT_tile(i)
                lower(i)
                hidden(i)
                y_tile(i)
            overflow_loop(dve, over)

            for i in range(KD // 2):
                dve.wait_ge(a_half, A_OUT + i + 1)
                dve.wait_ge(d_pg, 16)
                dve.tensor_tensor(pg_lo[i], w_pg[:, 2 * i:2 * i + 2], pg_hi[i].bitcast(f32), ALU.subtract).then_inc(v_half, 1)

            def combine(t, k):
                c = PAIRS * t + k
                dve.wait_ge(d_y[c % 4], 16 * (c // 4 + 1))
                if k:
                    dve.wait_ge(v_comb, c)
                for j in range(2):
                    w = wj[:, t, 2 * k + j:2 * k + j + 1]
                    ins = dve.scalar_tensor_tensor(x_sb[:, t], y_in[c % 4][:, j], w, x_sb[:, t], ALU.mult, ALU.add)
                    if j == 0:
                        link(ins)
                ins.then_inc(v_comb, 1)

            for k in range(PAIRS):
                combine(0, k)
            for t in range(NT):
                if t + 1 < NT:
                    combine(t + 1, 0)
                dve.wait_ge(p_rs, 2 * NT + t + 1)
                dve.wait_ge(d_ple, 32)
                if t >= 2:
                    dve.wait_ge(pe_h3T, 2 * t - 2)
                dve.scalar_tensor_tensor(h3[:, t % 2], x_sb[:, t], rs[:, t:t + 1], g_ple_b, ALU.mult, ALU.mult).then_inc(v_h3, 1)
                if t + 1 < NT:
                    combine(t + 1, 1)
                if t:
                    dve.wait_ge(pe_pg, 2 * t)
                for hf in range(2):
                    dve.wait_ge(a_h3T, 2 * t + hf + 1)
                    dve.tensor_tensor(h3_lo[:, 4 * hf:4 * hf + 4], bank[2 * (t % 2) + hf][:].rearrange("p (c q) -> p c q", q=P),
                                      h3_hi[t % 2][:, 4 * hf:4 * hf + 4].bitcast(f32), ALU.subtract).then_inc(v_half, 1)
                for k in range(2, PAIRS) if t + 1 < NT else ():
                    combine(t + 1, k)
            t = NT - 1
            dve.wait_ge(p_out, t - 1)
            dve.wait_ge(d_out[1], 16)
            dve.wait_ge(d_ppi, 16)
            for hf in range(2):
                sl = slice(hf * BANK, (hf + 1) * BANK)
                dve.wait_ge(pe_pg, 2 * t + hf + 1)
                dve.tensor_tensor(gate3[:, 1, sl], bank[4 + 2 * (t % 2) + hf][:], b_ple_b[:, sl], ALU.add).then_inc(v_gb, 1)
            for hf in range(2):
                sl = slice(hf * BANK, (hf + 1) * BANK)
                dve.wait_ge(a_gate, t + hf + 1)
                link(dve.tensor_tensor(out_st[:, 1, sl], gate3[:, 1, sl], pp_in[:, t, sl], ALU.mult))
                dve.tensor_tensor(out_st[:, 1, sl], out_st[:, 1, sl], x_sb[:, t, sl], ALU.add).then_inc(v_out, 1)

        @block.tensor
        def _(pe):
            mm, tp = pe.matmul, pe.transpose

            pe.wait_ge(p_pos, 1)
            tp(bank[7][:, 0:2 * KD], rows[:], ident[0:2 * KD, 0:2 * KD])
            tp(bank[7][:, 2 * KD:2 * KD + NT], pos_f[:], ident[0:NT, 0:NT]).then_inc(pe_rows, 1)
            pe.wait_ge(d_p, 32)
            pe.wait_ge(v_cols, 1)
            for t in range(NT):
                for c in range(2):
                    ins = tp(bank[4 + t][:, c * P:(c + 1) * P], p_sb[:, t, c * P:(c + 1) * P], ident[:])
                ins.then_inc(pe_pT, 1)
            for t in range(NT):
                pe.wait_ge(a_pT, t + 1)
                if t >= 2:
                    pe.wait_ge(a_pp, t - 1)
                    pe.wait_ge(v_pp, t - 1)
                for hf in range(2):
                    for c in range(2):
                        ins = mm(bank[2 * (t % 2) + hf][:], pT[:, c, tsl(t)], w_pp[:, c, hf * BANK:(hf + 1) * BANK],
                                 start=c == 0, stop=c == 1)
                ins.then_inc(pe_pp, 1)
            pe.wait_ge(a_pT, NT)
            for t in range(NT):
                pe.wait_ge(v_xn, t + 1)
                if t >= 2:
                    pe.wait_ge(a_hT, t - 1)
                    pe.wait_ge(v_hT, t - 1)
                for k in range(KD):
                    ins = tp(bank[4 + 2 * (t % 2) + k // 4][:, (k % 4) * P:(k % 4 + 1) * P], xn[:, t % 2, tsl(k)], ident[:])
                    if k % 4 == 3:
                        ins.then_inc(pe_hT, 1)

            def z_tile(t):
                for k in range(KD):
                    pe.wait_ge(d_w1[k // 2], 32)
                    for c in range(3):
                        ins = mm(bank[3 * (t % 2) + c][:, 0:Z_CHUNK], hT[:, k, tsl(t)], w1[:, k, c * Z_CHUNK:(c + 1) * Z_CHUNK],
                                 start=k == 0, stop=k == KD - 1)
                ins.then_inc(pe_z, 1)

            def cT_tile(t):
                pe.wait_ge(v_cn, t + 1)
                if t:
                    pe.wait_ge(a_cT, t)
                    pe.wait_ge(v_cT, t)
                for c in range(C_BLOCKS):
                    dst = bank[6][:, c * P:(c + 1) * P] if c < 4 else bank[7][:, 0:P]
                    ins = tp(dst, c_n[:, t % 2, c * P:(c + 1) * P], ident[:])
                ins.then_inc(pe_cT, 1)

            def up_tile(t):
                if t:
                    pe.wait_ge(a_up, 2 * t)
                    pe.wait_ge(v_up, 2 * t)
                n = MH * QK // 2
                for hf in range(2):
                    for c in range(Q_BLOCKS):
                        mm(bank[hf][:, 0:n], cT[:, c, tsl(t)], wuq[:, c, hf * n:(hf + 1) * n], start=c == 0, stop=c == Q_BLOCKS - 1)
                for hf in range(2):
                    for c in range(2):
                        ins = mm(bank[2 + hf][:], cT[:, Q_BLOCKS + c, tsl(t)], wukv[:, c, hf * BANK:(hf + 1) * BANK],
                                 start=c == 0, stop=c == 1)
                ins.then_inc(pe_up, 1)

            def gate(c):
                g, cols_of = c // 2, slice((c % 2) * P, (c % 2 + 1) * P)
                if c >= 2:
                    pe.wait_ge(a_g, c - 1)
                if c < SPLIT_GATE:
                    pe.wait_ge(d_wg[g % 2], 16 * (g // 2 + 1))
                    for k in range(KD):
                        ins = mm(bank[4 + c % 2][:], w_g[g % 2][:, k, cols_of], hT[:, k, :], start=k == 0, stop=k == KD - 1)
                else:
                    upper = [h_hi[k // 4][:, k % 4] for k in range(KD)]
                    lower = [h_lo[0][:, k] for k in range(3)] + [h_lo[1][:, k] for k in range(2)] + [h_lo[2][:, k] for k in range(3)]
                    pe.wait_ge(a_half, 2 + c - SPLIT_GATE + 1)
                    for n in range(3):
                        if n == 1:
                            pe.wait_ge(v_half, 3 + c - SPLIT_GATE + 1 + (c >= SPLIT_GATE + 2))
                        if n == 2 and c == SPLIT_GATE:
                            pe.wait_ge(v_half, 6)
                        for k in range(KD):
                            w = wg_lo[g % 2][:, k, cols_of] if n == 1 else wg_hi[c % 2][:, k]
                            ins = mm(bank[4 + c % 2][:], w, lower[k] if n == 2 else upper[k], start=n + k == 0, stop=n == 2 and k == KD - 1)
                ins.then_inc(pe_g, 1)

            for s_, n_ in ((a_hT, NT), (v_hT, NT), (a_pp, NT), (v_pp, NT)):
                pe.wait_ge(s_, n_)
            z_tile(0); z_tile(1); cT_tile(0)
            pe.wait_ge(a_z, 2); pe.wait_ge(v_z, 1)
            z_tile(2); cT_tile(1)
            pe.wait_ge(a_z, 4); pe.wait_ge(v_z, 2)
            z_tile(3); cT_tile(2)
            pe.wait_ge(a_z, 2 * NT); pe.wait_ge(v_z, NT)
            gate(0); cT_tile(3)
            pe.wait_ge(a_cT, NT); pe.wait_ge(v_cT, NT); pe.wait_ge(d_wu, 32)
            for t in range(NT):
                up_tile(t)
                if t < 3:
                    gate(t + 1)
            for c in range(4, 2 * KD):
                gate(c)

            pe.wait_ge(v_nrm, NT)
            pe.wait_ge(p_prep, NT)
            for j in range(22):
                if j == 0:
                    pe.wait_ge(a_up, 2 * NT); pe.wait_ge(v_up, 2 * NT)
                if j >= 4:
                    pe.wait_ge((a_tr, v_tr)[j % 2], (j - 4) // 2 + 1)
                for t in range(NT):
                    if j < 8:
                        src = q_sb[:, t, j * QK:(j + 1) * QK]
                    elif j < 16:
                        src = kk[:, t, (j - 8) * QK:(j - 7) * QK]
                    elif j < 20:
                        src = z[:, t, C_QS + (j - 16) * P:C_QS + (j - 15) * P]
                    else:
                        src = k_dup[:, t, (j - 20) * P:(j - 19) * P]
                    ins = tp(bank[j % 4][0:src.shape[1], tsl(t)], src, ident[:])
                ins.then_inc(pe_tr, 1)

            pe.wait_ge(a_tr, 11); pe.wait_ge(v_tr, 11); pe.wait_ge(a_g, 2 * KD)

            def scores(u):
                qt, kind, h = units[u]
                if u >= 3:
                    pe.wait_ge(a_e, u - 2)
                b = bank[u % 3]
                if kind == 0:
                    ins = mm(b[:], qT[0:QK, h, tsl(qt)], kT[0:QK, h], start=True, stop=True)
                else:
                    lo, n = band(qt)
                    r = slice(HD * (h % 2), HD * (h % 2) + HD)
                    masks = ([(0, 0)] if qt > 0 else []) + ([(n - 1, 1)] if qt < NT - 1 else [])
                    mm(b[:, 0:n * P], qwT[r, h // 2, tsl(qt)], kwT[r, h // (WH // WKV), lo * P:(lo + n) * P],
                       start=True, stop=False)
                    for x_, (blk, m) in enumerate(masks):
                        ins = mm(b[:, blk * P:(blk + 1) * P], ident_b[:], band_b[:, m], start=False, stop=x_ == len(masks) - 1)
                ins.then_inc(pe_s, 1)

            def transposes(u):
                qt, kind, h = units[u]
                pe.wait_ge(a_e, u + 1)
                if u >= 2:
                    pe.wait_ge((a_pt, v_pt)[u % 2], (u - 2) // 2 + 1)
                for b in range(NT if kind == 0 else band(qt)[1]):
                    ins = tp(bank[3 + u % 2][:, tsl(b)], prob[:, u % 2, tsl(b)], ident[:])
                ins.then_inc(pe_t, 1)

            def values(u):
                qt, kind, h = units[u]
                g = u // 8
                pe.wait_ge((a_pt, v_pt)[u % 2], u // 2 + 1)
                if h == 0 and g >= 2:
                    pe.wait_ge(v_o, g - 1)
                lo, n = (0, NT) if kind == 0 else band(qt)
                for b in range(n):
                    v = (kv[:, lo + b, h * (NOPE + VD) + NOPE:(h + 1) * (NOPE + VD)] if kind == 0 else
                         z[:, lo + b, C_VS + HD * (h // (WH // WKV)):C_VS + HD * (h // (WH // WKV) + 1)])
                    ins = mm(bank[5 + g % 2][:, h * VD:(h + 1) * VD], probT[:, u % 2, tsl(b)], v, start=b == 0, stop=b == n - 1)
                ins.then_inc(pe_pv, 1)

            def out_transposes(g):
                pe.wait_ge(v_o, g + 1)
                if g:
                    pe.wait_ge(a_oT, g)
                for c in range(4):
                    ins = tp(bank[7][:, tsl(c)], o_sb[:, tsl(c)], ident[:])
                ins.then_inc(pe_ot, 1)

            for i in range(UNITS + 16):
                if i < UNITS:
                    scores(i)
                if 0 <= i - 2 < UNITS:
                    transposes(i - 2)
                if 0 <= i - 3 < UNITS:
                    values(i - 3)
                if i >= 12 and (i - 12) % 8 == 0 and (i - 12) // 8 < 2 * NT:
                    out_transposes((i - 12) // 8)

            pe.wait_ge(a_oT, 2 * NT)
            pe.wait_ge(d_br, 32)
            for c in range(KD):
                if c >= 2:
                    pe.wait_ge(v_br, c - 1)
                for w, o, b in ((w_bm, oT_m, bank[c % 2]), (w_bs, oT_w, bank[2 + c % 2])):
                    for k in range(4):
                        ins = mm(b[:], w[:, k, tsl(c)], o[:, k], start=k == 0, stop=k == 3)
                ins.then_inc(pe_br, 1)

            def h2_transposes(t):
                pe.wait_ge(v_h2, t + 1)
                if t >= 2:
                    pe.wait_ge(a_h2T, t - 1)
                    pe.wait_ge(v_h2T, t - 1)
                for k in range(KD):
                    ins = tp(bank[2 * (t % 2) + k // 4][:, (k % 4) * P:(k % 4 + 1) * P], h2[:, t % 2, tsl(k)], ident[:])
                    if k % 4 == 3:
                        ins.then_inc(pe_h2T, 1)

            for t in range(NT):
                if t >= 2:
                    pe.wait_ge(v_x1, 2 * (t - 1))
                for n, (m, w) in enumerate(((m_hi, wo_hi), (m_hi, wo_lo), (m_lo, wo_hi))):
                    if t == 0 and n == 1:
                        pe.wait_ge(v_half, V_OUT)
                    for k in range(KD):
                        if t == 0 and n == 0:
                            pe.wait_ge(a_half, A_GATES + min(2 * k + 2, k + 1 + KD // 2))
                        for hf in range(2):
                            ins = mm(bank[4 + 2 * (t % 2) + hf][:], m[k][:, tsl(t)], w[k // 2][:, k % 2, hf * BANK:(hf + 1) * BANK],
                                     start=n + k == 0, stop=n == 2 and k == KD - 1)
                ins.then_inc(pe_wo, 1)
                if t:
                    h2_transposes(t - 1)
            pe.wait_ge(d_wr, 48)

            def logits(t):
                pe.wait_ge(a_h2T, t + 1); pe.wait_ge(v_h2T, t + 1)
                if t == 0:
                    pe.wait_ge(v_x1, 2 * (NT - 1))
                for k in range(KD):
                    ins = mm(bank[4][:, t * E:(t + 1) * E], h2T[:, k, tsl(t)], w_r[:, k], start=k == 0, stop=k == KD - 1)
                return ins

            for t in range(NT - 2):
                logits(t)
            h2_transposes(NT - 1)
            logits(NT - 2)
            logits(NT - 1).then_inc(pe_lg, 1)
            pe.wait_ge(v_x1, 2 * NT)
            pe.wait_ge(d_sg, 16)
            for c in range(4):
                for k in range(KD):
                    ins = mm(bank[(5, 6, 7, 0)[c]][:], w_sg[:, k, tsl(c)], h2T[:, k], start=k == 0, stop=k == KD - 1)
                ins.then_inc(pe_sh, 1)
            pe.wait_ge(v_mask, 1)
            pe.wait_ge(a_ssh, 2); pe.wait_ge(v_sh, 2)
            pe.wait_ge(d_sd, 16)
            for t in range(NT):
                for s in range(t + 1):
                    ins = mm(bank[6][:, t * E:(t + 1) * E], (before_b if s == t else ones_b)[:], mask_b[:, s], start=s == 0, stop=s == t)
            for t in range(NT):
                ins = mm(bank[6][0:E, COUNTS:COUNTS + 1], mask_b[:, t], ones_b[:, 0:1], start=t == 0, stop=t == NT - 1)
            ins.then_inc(pe_rank, 1)
            def table_starts():
                pe.wait_ge(v_more, 1)
                mm(bank[6][0:E, COUNTS + 1:COUNTS + 2], before_b[0:E, 0:E], more_b[:, 0:1], start=True, stop=True)
                mm(bank[6][0:1, COUNTS + 2:COUNTS + 3], more_b[:, 0:1], ones_b[0:E, 0:1], start=True, stop=True).then_inc(pe_st, 1)

            def table_rows():
                pe.wait_ge(v_hot, 1)
                for w in range(2):
                    for k in range(1, TILES_MAX):
                        c = 0 if w == 0 else k
                        ins = mm(bank[6][0:1, TABLE + E * w:TABLE + E * (w + 1)], tab_t[0:E, TILES_MAX - 1, c:c + 1], tab_t[0:E, k - 1],
                                 start=k == 1, stop=k == TILES_MAX - 1)
                ins.then_inc(pe_tab, 1)

            def early(i, n):
                return isinstance(i.n, int) and i.n < n

            def info_of(i):
                pe.wait_ge(v_oh, i.n + 1)
                if not early(i, 1):
                    pe.wait_ge(v_idx, i.n)
                for a_ in range(NT):
                    ins = mm(bank[7][0:SLOTS, 0:8], onehot[:, i.s2, a_], info_t[:, i.s2, a_ * 8:(a_ + 1) * 8], start=a_ == 0, stop=a_ == NT - 1)
                ins.then_inc(pe_info, 1)

            def turn(i):
                pe.wait_ge(d_xg[i.s4], 16 * i.uses4)
                if not early(i, 1):
                    pe.wait_ge(a_xT, i.n)
                    pe.wait_ge(v_xT, i.n)
                for k in range(KD):
                    ins = tp(bank[k // 4][:, (k % 4) * SLOTS:(k % 4 + 1) * SLOTS], xg[i.s4][0:SLOTS, tsl(k)], ident[0:SLOTS, 0:SLOTS])
                ins.then_inc(pe_T, 1)

            def gate_up(i):
                pe.wait_ge(a_xT, i.n + 1)
                pe.wait_ge(v_xT, i.n + 1)
                pe.wait_ge(d_gu[i.s4], 16 * i.uses4)
                if not early(i, 2):
                    pe.wait_ge(v_hid, i.n - i.lag2 + 1)
                for c in range(4):
                    for k in range(KD):
                        ins = mm(bank[2 + i.s2][:, c * SLOTS:(c + 1) * SLOTS], w_gu[i.s4][:, k, tsl(c)], xT[:, i.s2, k], start=k == 0, stop=k == KD - 1)
                ins.then_inc(pe_gu, 1)

            def down(i):
                pe.wait_ge(v_hid, i.n + 1)
                pe.wait_ge(v_lo, i.n + 1)
                if not early(i, 1):
                    pe.wait_ge(a_y, i.n)
                    pe.wait_ge(v_y, i.n)
                parts = ((hid_hi, w_hi[i.s2]), (hid_hi, w_lo[i.s4]), (hid_lo, w_hi[i.s2]))
                for hf in range(2):
                    for n, (hid, w) in enumerate(parts):
                        for c in range(2):
                            ins = mm(bank[4 + hf][0:SLOTS, :], hid[:, i.s2, c], w[:, c, hf * BANK:(hf + 1) * BANK],
                                     start=n + c == 0, stop=n + c == 3)
                ins.then_inc(pe_dn, 1)

            def step(i):
                if shift(i, 3) is not None:
                    info_of(shift(i, 3))
                gate_up(i)
                if shift(i, 1) is not None:
                    turn(shift(i, 1))
                if shift(i, -1) is not None:
                    down(shift(i, -1))
            def shared_down(b, t, hf):
                for c in range(2):
                    ins = mm(bank[b][:], shT[:, c, tsl(t)], w_sd[:, c, hf * BANK:(hf + 1) * BANK], start=c == 0, stop=c == 1)
                return ins

            for t in range(2):
                for hf in range(2):
                    ins = shared_down(((1, 2), (3, 5))[t][hf], t, hf)
                ins.then_inc(pe_sd, 1)
                info_of(item(0, t))
            info_of(item(0, 2))
            pe.wait_ge(v_base, 2)
            turn(item(0, 0))
            for n in range(GROUP):
                if n == 1:
                    pe.wait_ge(v_base, 4)
                step(item(0, n))
                if n == 1:
                    table_starts()
                if n == 2:
                    table_rows()
                u = n - (GROUP - LATE)
                if u >= 0:
                    pe.wait_ge(v_tab, 3) if u == 0 else pe.wait_ge(v_base, 4 + u)
                    shared_down(6, 2 + u // 2, u % 2).then_inc(pe_sd, 1)
            item_loop(pe, step, GROUP, E - GROUP)
            for n in range(E - GROUP, E):
                step(item(0, n))
            down(item(0, E - 1))

            def over(i, j):
                info_of(i)
                turn(i)
                gate_up(i)
                down(i)
            overflow_loop(pe, over)

            for t in range(NT):
                pe.wait_ge(v_h3, t + 1)
                if t >= 2:
                    pe.wait_ge(v_half, V_OUT + KD // 2 + 2 * t - 2)
                for k in range(KD):
                    ins = tp(bank[2 * (t % 2) + k // 4][:, (k % 4) * P:(k % 4 + 1) * P], h3[:, t % 2, tsl(k)], ident[:])
                    if k % 4 == 3:
                        ins.then_inc(pe_h3T, 1)
                pe.wait_ge(a_h3T, 2 * t + 2)
                pe.wait_ge(v_half, V_OUT + KD // 2)
                if t >= 2:
                    pe.wait_ge(a_pg, 2 * t - 2)
                for hf in range(2):
                    for n, (h, w) in enumerate(((h3_hi[t % 2], pg_hi), (h3_hi[t % 2], pg_lo), (h3_lo, pg_hi))):
                        if n == 2:
                            pe.wait_ge(v_half, V_OUT + KD // 2 + 2 * t + 2)
                        for k in range(KD):
                            ins = mm(bank[4 + 2 * (t % 2) + hf][:], h[:, k], w[k // 2][:, k % 2, hf * BANK:(hf + 1) * BANK],
                                     start=n + k == 0, stop=n == 2 and k == KD - 1)
                    ins.then_inc(pe_pg, 1)


_INS = ["x", "p", "positions", "g_mix", "w_in", "b_gate", "g_cq", "w_uq", "g_ckv", "w_ukv", "g_qn_mla", "g_kn_mla",
        "g_qn_swa", "g_kn_swa", "sink", "w_br_mla", "w_br_swa", "w_out", "g_moe", "w_router", "router_bias",
        "w_exp_gu", "w_exp_down", "w_sh_gu", "w_sh_down", "g_ple", "w_ple_gate", "b_ple", "w_ple_proj"]


def kernel(**inputs):
    import numpy as _np
    import concourse.bacc as _bacc
    from concourse import mybir as _mybir
    from concourse.bass_utils import run_bass_kernel_spmd as _run

    nc = _bacc.Bacc("TRN2", target_bir_lowering=False, num_devices=1)
    arrays, args = {}, []
    for name in _INS:
        arrays[f"in_{name}"] = _np.ascontiguousarray(inputs[name])
    arrays["in_rope_freq"] = _np.concatenate([
        _np.float32(1.0) / _np.float32(THETA) ** (_np.arange(0, n, 2, dtype=_np.float32) / _np.float32(n))
        for n in (ROPE, HD)]).astype(_np.float32).reshape(1, NF)
    for name, a in arrays.items():
        args.append(nc.dram_tensor(name, a.shape, _mybir.dt.from_np(a.dtype), kind="ExternalInput").ap())
    args.append(nc.dram_tensor("out_0", (1, T, D), _mybir.dt.float32, kind="ExternalOutput").ap())
    build(nc, *args)
    r = _run(nc, [arrays], core_ids=[0])
    return r.results[0]["out_0"]
```
